# Optimizing a Trainium2 kernel written in Bass

```python
import math
import jax, jax.numpy as jnp
from jax import lax
import numpy as np

D_MODEL = 1024
BATCH = 1
SEQ = 256
DEPTH = 1
DEC_BATCH = 8
DEC_SEQ = 1
PAST_LEN = 2048
PAGE_SIZE = 128

N_HEADS = 8
HEAD_DIM = 64
ATTN_WIDTH = N_HEADS * HEAD_DIM
CONV_CH = D_MODEL // 2
CONV_WIDTH = 31
MOBA_BLOCK = 256
MOBA_TOPK = 3
Q_CHUNK = 16
D_FF = ((8 * D_MODEL // 3 + 255) // 256) * 256
EPS = 1e-6
NEG = -1e30

kernel_name = 'moba_conformer_hybrid_step'

def rms_norm(x, g):
    xf = x.astype(jnp.float32)
    y = xf * lax.rsqrt(jnp.mean(xf * xf, axis=-1, keepdims=True) + EPS)
    return (y * g.astype(jnp.float32)).astype(x.dtype)

def layer_norm(x, g, b):
    xf = x.astype(jnp.float32)
    mu = jnp.mean(xf, axis=-1, keepdims=True)
    var = jnp.mean(jnp.square(xf - mu), axis=-1, keepdims=True)
    y = (xf - mu) * lax.rsqrt(var + EPS)
    return (y * g.astype(jnp.float32) + b.astype(jnp.float32)).astype(x.dtype)

def alibi_slopes():
    return jnp.exp2(-8.0 * jnp.arange(1, N_HEADS + 1, dtype=jnp.float32) / N_HEADS)

def moba_attention(q, k, v, q_offset, slopes):
    B, Sq, H, Dh = q.shape
    T = k.shape[1]
    nb = -(-T // MOBA_BLOCK)
    pad = nb * MOBA_BLOCK - T
    kp = jnp.pad(k, ((0, 0), (0, pad), (0, 0), (0, 0)))
    vp = jnp.pad(v, ((0, 0), (0, pad), (0, 0), (0, 0)))
    kb = kp.reshape(B, nb, MOBA_BLOCK, H, Dh)
    vb = vp.reshape(B, nb, MOBA_BLOCK, H, Dh)
    k_mean = jnp.mean(kb.astype(jnp.float32), axis=2)
    t_q = q_offset + jnp.arange(Sq, dtype=jnp.int32)
    q_blk = t_q // MOBA_BLOCK
    gate = jnp.einsum('bshd,bnhd->bhsn', q.astype(jnp.float32), k_mean)
    fully_past = jnp.arange(nb, dtype=jnp.int32)[None, :] < q_blk[:, None]
    gate = jnp.where(fully_past[None, None], gate, NEG)
    ks = min(MOBA_TOPK, nb)
    _, idx = lax.top_k(gate, ks)
    qc = math.gcd(Q_CHUNK, Sq)
    nc = Sq // qc
    bi = jnp.arange(B)[:, None, None, None]
    hi = jnp.arange(H)[None, :, None, None]
    scale = Dh ** -0.5
    j_pos = jnp.arange(MOBA_BLOCK, dtype=jnp.int32)

    def chunk(ci):
        s0 = ci * qc
        q_c = lax.dynamic_slice_in_dim(q, s0, qc, axis=1).astype(jnp.float32) * scale
        idx_c = lax.dynamic_slice_in_dim(idx, s0, qc, axis=2)
        t_c = q_offset + s0 + jnp.arange(qc, dtype=jnp.int32)
        blk_c = t_c // MOBA_BLOCK
        k_sel = kb[bi, idx_c, :, hi].astype(jnp.float32)
        v_sel = vb[bi, idx_c, :, hi].astype(jnp.float32)
        s_sel = jnp.einsum('bqhd,bhqnjd->bhqnj', q_c, k_sel)
        pos_sel = idx_c[..., None] * MOBA_BLOCK + j_pos
        ok_sel = idx_c[..., None] < blk_c[None, None, :, None, None]
        dist_sel = (t_c[None, None, :, None, None] - pos_sel).astype(jnp.float32)
        s_sel = jnp.where(ok_sel, s_sel - slopes[None, :, None, None, None] * dist_sel, NEG)
        own0 = ((q_offset + s0) // MOBA_BLOCK) * MOBA_BLOCK
        k_own = lax.dynamic_slice_in_dim(kp, own0, MOBA_BLOCK, axis=1).astype(jnp.float32)
        v_own = lax.dynamic_slice_in_dim(vp, own0, MOBA_BLOCK, axis=1).astype(jnp.float32)
        s_own = jnp.einsum('bqhd,bjhd->bhqj', q_c, k_own)
        dist_own = (t_c[:, None] - (own0 + j_pos)[None, :]).astype(jnp.float32)
        s_own = jnp.where(dist_own[None, None] >= 0.0,
                          s_own - slopes[None, :, None, None] * dist_own[None, None], NEG)
        scores = jnp.concatenate([s_sel.reshape(B, H, qc, ks * MOBA_BLOCK), s_own], axis=-1)
        p = jax.nn.softmax(scores, axis=-1)
        p_sel = p[..., :ks * MOBA_BLOCK].reshape(B, H, qc, ks, MOBA_BLOCK)
        p_own = p[..., ks * MOBA_BLOCK:]
        o = (jnp.einsum('bhqnj,bhqnjd->bqhd', p_sel, v_sel)
             + jnp.einsum('bhqj,bjhd->bqhd', p_own, v_own))
        return o.astype(q.dtype)

    out = lax.map(chunk, jnp.arange(nc, dtype=jnp.int32))
    return out.transpose(1, 0, 2, 3, 4).reshape(B, Sq, H * Dh)

def depthwise_causal_conv(buf, w):
    return lax.conv_general_dilated(buf, w, window_strides=(1,), padding='VALID',
                                    dimension_numbers=('NWC', 'WIO', 'NWC'),
                                    feature_group_count=CONV_CH)

def hybrid_layer(x, c, k_past, v_past, conv_past, pos0, w_ada, b_ada, g_norm1, w_in, g_q, g_k,
                 w_attn_proj, w_dwconv, b_dwconv, g_conv_ln, b_conv_ln, w_conv_proj, w_out,
                 g_norm2, w_ffn_in, w_ffn_out):
    B, S, _ = x.shape
    mod = jax.nn.silu(c) @ w_ada + b_ada
    sh1, sc1, gt1, sh2, sc2, gt2 = [m[:, None, :] for m in jnp.split(mod, 6, axis=-1)]
    h = rms_norm(x, g_norm1) * (1.0 + sc1) + sh1
    proj = h @ w_in
    A, C, D = ATTN_WIDTH, CONV_CH, D_MODEL
    q, k, v, glu_a, glu_b, gate_a, gate_c = jnp.split(
        proj, [A, 2 * A, 3 * A, 3 * A + C, 3 * A + 2 * C, 3 * A + 2 * C + D], axis=-1)
    q = rms_norm(q.reshape(B, S, N_HEADS, HEAD_DIM), g_q)
    k = rms_norm(k.reshape(B, S, N_HEADS, HEAD_DIM), g_k)
    v = v.reshape(B, S, N_HEADS, HEAD_DIM)
    k_all = jnp.concatenate([k_past, k], axis=1)
    v_all = jnp.concatenate([v_past, v], axis=1)
    attn = moba_attention(q, k_all, v_all, pos0, alibi_slopes()) @ w_attn_proj
    u = glu_a * jax.nn.sigmoid(glu_b)
    conv_in = jnp.concatenate([conv_past, u], axis=1)
    cv = depthwise_causal_conv(conv_in, w_dwconv) + b_dwconv
    cv = jax.nn.silu(layer_norm(cv, g_conv_ln, b_conv_ln)) @ w_conv_proj
    mix = (jax.nn.sigmoid(gate_a) * attn + jax.nn.sigmoid(gate_c) * cv) @ w_out
    x = x + gt1 * mix
    h2 = rms_norm(x, g_norm2) * (1.0 + sc2) + sh2
    f_g, f_u = jnp.split(h2 @ w_ffn_in, 2, axis=-1)
    x = x + gt2 * ((jax.nn.silu(f_g) * f_u) @ w_ffn_out)
    return x, k, v, conv_in[:, -(CONV_WIDTH - 1):]

def setup_inputs(seed: int = 0) -> dict:
    key = jax.random.key(seed)
    ks = jax.random.split(key, 24)
    f32 = jnp.float32
    n_pages = PAST_LEN // PAGE_SIZE
    n_used = DEC_BATCH * n_pages
    n_phys = n_used + max(1, n_used // 4)
    nrm = lambda k, shape, s: jax.random.normal(k, shape, f32) * s
    page_table = jax.random.permutation(ks[0], n_phys)[:n_used].reshape(DEC_BATCH, n_pages).astype(jnp.int32)
    w_in_cols = 3 * ATTN_WIDTH + 2 * CONV_CH + 2 * D_MODEL
    return {
        'x_prompt': nrm(ks[1], (BATCH, SEQ, D_MODEL), 1.0),
        'x_sample': nrm(ks[2], (DEC_BATCH, DEC_SEQ, D_MODEL), 1.0),
        'cache_k': nrm(ks[3], (n_phys, PAGE_SIZE, N_HEADS, HEAD_DIM), 1.0),
        'cache_v': nrm(ks[4], (n_phys, PAGE_SIZE, N_HEADS, HEAD_DIM), 1.0),
        'state_conv': nrm(ks[5], (DEC_BATCH, CONV_WIDTH - 1, CONV_CH), 0.5),
        'page_table': page_table,
        'c_prompt': nrm(ks[6], (BATCH, D_MODEL), 1.0),
        'c_sample': nrm(ks[7], (DEC_BATCH, D_MODEL), 1.0),
        'w_ada': nrm(ks[8], (D_MODEL, 6 * D_MODEL), 0.5 * D_MODEL ** -0.5),
        'b_ada': nrm(ks[9], (6 * D_MODEL,), 0.01),
        'g_norm1': 1.0 + nrm(ks[10], (D_MODEL,), 0.02),
        'w_in': nrm(ks[11], (D_MODEL, w_in_cols), D_MODEL ** -0.5),
        'g_q': 1.0 + nrm(ks[12], (HEAD_DIM,), 0.02),
        'g_k': 1.0 + nrm(ks[13], (HEAD_DIM,), 0.02),
        'w_attn_proj': nrm(ks[14], (ATTN_WIDTH, D_MODEL), ATTN_WIDTH ** -0.5),
        'w_dwconv': nrm(ks[15], (CONV_WIDTH, 1, CONV_CH), CONV_WIDTH ** -0.5),
        'b_dwconv': nrm(ks[16], (CONV_CH,), 0.01),
        'g_conv_ln': 1.0 + nrm(ks[17], (CONV_CH,), 0.02),
        'b_conv_ln': nrm(ks[18], (CONV_CH,), 0.01),
        'w_conv_proj': nrm(ks[19], (CONV_CH, D_MODEL), CONV_CH ** -0.5),
        'w_out': nrm(ks[20], (D_MODEL, D_MODEL), D_MODEL ** -0.5),
        'g_norm2': 1.0 + nrm(ks[21], (D_MODEL,), 0.02),
        'w_ffn_in': nrm(ks[22], (D_MODEL, 2 * D_FF), D_MODEL ** -0.5),
        'w_ffn_out': nrm(ks[23], (D_FF, D_MODEL), D_FF ** -0.5),
    }

def reference(x_prompt, x_sample, cache_k, cache_v, state_conv, page_table, c_prompt, c_sample,
              w_ada, b_ada, g_norm1, w_in, g_q, g_k, w_attn_proj, w_dwconv, b_dwconv,
              g_conv_ln, b_conv_ln, w_conv_proj, w_out, g_norm2, w_ffn_in, w_ffn_out):
    weights = (w_ada, b_ada, g_norm1, w_in, g_q, g_k, w_attn_proj, w_dwconv, b_dwconv,
               g_conv_ln, b_conv_ln, w_conv_proj, w_out, g_norm2, w_ffn_in, w_ffn_out)
    B = x_prompt.shape[0]
    DB = x_sample.shape[0]
    k_past0 = jnp.zeros((B, 0, N_HEADS, HEAD_DIM), x_prompt.dtype)
    v_past0 = jnp.zeros((B, 0, N_HEADS, HEAD_DIM), x_prompt.dtype)
    conv0 = jnp.zeros((B, CONV_WIDTH - 1, CONV_CH), x_prompt.dtype)
    y_prompt = x_prompt
    for _ in range(DEPTH):
        y_prompt, k_prompt, v_prompt, conv_prompt = hybrid_layer(
            y_prompt, c_prompt, k_past0, v_past0, conv0, 0, *weights)
    k_past = cache_k[page_table].reshape(DB, -1, N_HEADS, HEAD_DIM)
    v_past = cache_v[page_table].reshape(DB, -1, N_HEADS, HEAD_DIM)
    y_sample = x_sample
    for _ in range(DEPTH):
        y_sample, k_sample, v_sample, conv_sample = hybrid_layer(
            y_sample, c_sample, k_past, v_past, state_conv, PAST_LEN, *weights)
    return (y_prompt, y_sample, k_prompt, v_prompt, conv_prompt, k_sample, v_sample, conv_sample)


_drawn_inputs = setup_inputs


def setup_inputs(seed=0):
    import zlib

    import numpy as np

    out = dict(_drawn_inputs(seed))
    spreads = {}
    factors = {'b_ada': 2.866,
     'g_norm1': 2.821,
     'g_q': 18.507,
     'g_k': 7.813,
     'b_dwconv': 8.0,
     'g_conv_ln': 23.495,
     'b_conv_ln': 48.583,
     'g_norm2': 8.0}
    for name, (base, spread) in spreads.items():
        noise = np.random.default_rng([zlib.crc32(name.encode()), seed]).standard_normal(out[name].shape)
        drawn = base * np.exp(spread * noise) if base else spread * noise
        out[name] = __import__('jax').numpy.asarray(drawn.astype(out[name].dtype))
    for name, factor in factors.items():
        out[name] = (out[name] * factor).astype(out[name].dtype)
    return out
```

```python
from contextlib import ExitStack

import concourse.bass as bass
from concourse import mybir

F32 = mybir.dt.float32
I32 = mybir.dt.int32
ALU = mybir.AluOpType
ACT = mybir.ActivationFunctionType
AX = mybir.AxisListType

P = 128
D = 1024
KD = D // P
S = 256
B = 8
R = S + B
H, DH = 8, 64
A = H * DH
AT = A // P
C = 512
CT = C // P
TAPS = 31
DFF = 2816
FT = DFF // P
PG = 16
CH = 4
PC = PG // CH
NB = 8
TOPK = 3
PAST = PG * P
NPHYS = 160
EPS = 1e-6
NEG = -1e30
FAR = 1e33
SLOT = 4096
RING = 3
PAIRS = B // 2

V_ADA, V_G1, V_G2, V_BDW, V_GLN, V_BLN, V_GQ, V_GK, V_ROWS = 0, 48, 56, 64, 68, 72, 76, 77, 78

ADA0, QKV0, GLU0, LOOP0 = 0, 4, 7, 9
CONV_W = LOOP0 + 3 * PAIRS
ATTN_W, OUT_W, FIN_W = CONV_W + 1, CONV_W + 2, CONV_W + 4
FOUT_W = FIN_W + FT // 2

PRE = (["vec", "x0", "x1", "x2", "x3", "x4", "x5", "x6", "x7", "c", "st0", "st1", "st2", "st3", "ss1",
        "ada0", "ada1", "adt0", "ada2", "adt1", "ada3", "adt2", "adt3"]
       + [f"q{t}" for t in range(4)] + [f"sqq{t}" for t in range(4)]
       + [f"k{t}" for t in range(4)] + ["qs"] + [f"sqk{t}" for t in range(4)]
       + [f"v{t}" for t in range(4)] + ["vn0", "vn1", "kn0", "kn1", "ks", "vs", "so"]
       + [f"a{t}" for t in range(4)] + [f"b{t}" for t in range(4)] + ["ct"])
PER_PAIR = 8
PAIR = ["ada0", "g0", "adt0", "g1", "g2", "ada1", "g3", "adt1"]
POST = (["lnm", "lnv"] + [f"cp{t}" for t in range(8)] + [f"ap{t}" for t in range(8)]
        + [f"o{t}" for t in range(8)] + ["ss2"]
        + [f"f{n}" for n in range(2 * FT)] + [f"y{t}" for t in range(8)]
        + ["y00", "y01", "y10", "y11", "y20", "y21"])
PRE_N = len(PRE)


def fill(name, i=None, k=0):
    if name == "pair":
        return PRE_N + k, i
    if name in PRE:
        return PRE.index(name), 0
    return PRE_N + PER_PAIR * PAIRS + POST.index(name), 0


def program(nc, x_prompt, x_sample, cache_k, cache_v, state_conv, page_table, c_prompt, c_sample,
            w_ada, b_ada, g_norm1, w_in, g_q, g_k, w_attn_proj, w_dwconv, b_dwconv,
            g_conv_ln, b_conv_ln, w_conv_proj, w_out, g_norm2, w_ffn_in, w_ffn_out,
            y_prompt, y_sample, k_prompt, v_prompt, conv_prompt, k_sample, v_sample, conv_sample):
    with ExitStack() as ctx:
        def sb(name, shape, dt=F32):
            return ctx.enter_context(nc.sbuf_tensor(name, shape, dt))

        def pb(name):
            return ctx.enter_context(nc.psum_tensor(name, [P, 512], F32))

        def sem(name):
            return ctx.enter_context(nc.semaphore(name))

        wring = sb("wring", [P, RING, SLOT])
        kring = sb("kring", [P, PG, A])
        vring = sb("vring", [P, PG, A])
        prod = sb("prod", [P, PC // 2, A])
        xT = sb("xT", [P, KD, R])
        hT = sb("hT", [P, KD, R])
        qkvT = sb("qkvT", [P, 12, R])
        qT, kT, vT = qkvT[:, 0:4, :], qkvT[:, 4:8, :], qkvT[:, 8:12, :]
        vnat = sb("vnat", [P, 2, A])
        u = sb("u", [P, CT, TAPS - 1 + R])
        cvT = sb("cvT", [P, CT, R])
        gates = sb("gates", [P, 16, R])
        oT = sb("oT", [P, AT, R])
        qst = sb("qst", [P, S])
        kst = sb("kst", [P, S])
        vst = sb("vst", [P, 2, P])
        pr = sb("pr", [P, 384])
        prT = sb("prT", [P, 384])
        sel = sb("sel", [B, P])
        snat = sb("snat", [B, A])
        ident = sb("ident", [P, P])
        ones = sb("ones", [P, P])
        halves = sb("halves", [P, P])
        distm = sb("distm", [P, 384])
        slopes = sb("slopes", [P, H])
        dists = sb("dists", [P, PG])
        alib = sb("alib", [P, PG, H])
        lower = sb("lower", [P, NB, NB])
        vt = sb("vt", [P, V_ROWS + TAPS * CT])
        vec = vt[:, 0:V_ROWS]
        taps = vt[:, V_ROWS:].rearrange("p (t c) -> p t c", c=CT)
        modT = sb("modT", [P, 48, B + 1])
        cT = sb("cT", [P, KD, 32])
        gs = sb("gs", [P, KD, B + 1])
        sall = sb("sall", [P, 2, PG, H])
        s1 = sb("s1", [P, PG + 1, H])
        sown = sb("sown", [P, B, H])
        ppad = sb("ppad", [P, PG, 32])
        pvm = sb("pvm", [P, A])
        headof = sb("headof", [P, H])
        mrow = sb("mrow", [P, 2, P])
        eps = sb("eps", [P, 1])
        diag = sb("diag", [H, PG, H])
        gate = sb("gate", [H, NB])
        cmp1 = sb("cmp1", [H, NB, NB])
        cmp2 = sb("cmp2", [H, NB, NB])
        tiny = sb("tiny", [P, 64])
        m1, nmx, dg, es, rinv, own = (tiny[:, 0:8], tiny[0:H, 8:9], tiny[0:H, 16:24], tiny[:, 24:32],
                                      tiny[:, 32:40], tiny[:, 40:44])
        pmx, psum_, prin = tiny[:, 48:50], tiny[:, 50:52], tiny[:, 52:54]
        cvs = sb("cvs", [P, CT, B])
        pages = sb("pages", [1, B * PG], I32)
        xn = vring[:, 0:6, :].rearrange("p (t k) n -> p t (k n)", t=3)
        cn = vring[0:B + 1, 6:8, :].rearrange("p k n -> p (k n)")
        stn = vring[0:120, 8:10, :]
        vecn = vring[0:V_ROWS, 10, 0:P]
        tapn = vring[0:TAPS * CT, 10, P:2 * P]
        ownp = cvT[0:B, 0:2, :].rearrange("p t r -> p (t r)")[:, 0:A]
        fT = kring[:, 0:12, :].rearrange("p a n -> p (a n)")[:, 0:FT * R].rearrange("p (t r) -> p t r", r=R)
        yn = vring[:, 0:6, :].rearrange("p (t k) n -> p t (k n)", t=3)
        knat = oT[:, :, :].rearrange("p t r -> p (t r)")[:, 0:2 * A].rearrange("p (t n) -> p t n", t=2)
        ctn = gates[0:TAPS - 1 + B, 0:2, :].rearrange("p t r -> p (t r)")[:, 0:C]
        skv = gates[0:B, 2:6, :].rearrange("p t r -> p (t r)")[:, 0:2 * A].rearrange("p (t n) -> p t n", t=2)
        rstd = prT[:, 0:R]
        soq = gates[0:B, 6, 0:2 * B * H].rearrange("p (t n) -> p t n", t=2)
        roots = [rstd, pr[:, 0:R]]
        tmp2 = cvT
        sq = gates[:, 0:8, :]

        acc = [pb("acc0"), pb("acc1")]
        qbc = [pb("qbc0"), pb("qbc1")]
        chain = pb("chain")
        psS = pb("psS")
        psT = pb("psT")
        psO = pb("psO")

        vec_in, x_in, c_in, st_in, pt_in = sem("vec_in"), sem("x_in"), sem("c_in"), sem("st_in"), sem("pt_in")
        w_full = [sem(f"w_full{n}") for n in range(RING)]
        w_used = sem("w_used")
        k_full = [sem(f"k_full{n}") for n in range(CH)]
        v_full = [sem(f"v_full{n}") for n in range(CH)]
        k_used, v_used = sem("k_used"), sem("v_used")
        consts = sem("consts")
        pool_step = sem("pool_step")
        acc_full = sem("acc_full")
        acc_free = [sem("acc_free0"), sem("acc_free1")]
        act_step, dve_step = sem("act_step"), sem("dve_step")
        c_silu, x_sq, h_ready, x_gone = sem("c_silu"), sem("x_sq"), sem("h_ready"), sem("x_gone")
        sq_ready, q_ready, k_ready = sem("sq_ready"), sem("q_ready"), sem("k_ready")
        so_ready, u_ready, nat_ready = sem("so_ready"), sem("u_ready"), sem("nat_ready")
        qsel_ready, qbc_ready = sem("qsel_ready"), sem("qbc_ready")
        scored = sem("scored")
        gs_ready, pen_ready, mask_ready, bias_ready = sem("gs_ready"), sem("pen_ready"), sem("mask_ready"), sem("bias_ready")
        m1_ready, m1t_ready, dg_ready, mb_ready = sem("m1_ready"), sem("m1t_ready"), sem("dg_ready"), sem("mb_ready")
        s2_ready, e_ready, es_ready, tot_ready = sem("s2_ready"), sem("e_ready"), sem("es_ready"), sem("tot_ready")
        p_ready, pvm_ready, pv_ready, o_ready = sem("p_ready"), sem("pvm_ready"), sem("pv_ready"), sem("o_ready")
        st_ready = sem("st_ready")
        ps_ready, pb_ready, pe_ready, pn_ready = sem("ps_ready"), sem("pb_ready"), sem("pe_ready"), sem("pn_ready")
        pt_ready, pc_ready, po_ready, pp_ready = sem("pt_ready"), sem("pc_ready"), sem("po_ready"), sem("pp_ready")
        ln_c, ln_s, cv_ready = sem("ln_c"), sem("ln_s"), sem("cv_ready")
        mix_ready, x2_ready, x2_sq, h2_ready = sem("mix_ready"), sem("x2_ready"), sem("x2_sq"), sem("h2_ready")
        silu_ready, f_ready, y_ready = sem("silu_ready"), sem("f_ready"), sem("y_ready")
        stored = sem("stored")

        block = ctx.enter_context(nc.Block())

        def when_full(eng, name, i=None, k=0):
            m, i = fill(name, i, k)
            eng.wait_ge(acc_full, m + 1 + PER_PAIR * i)
            return acc[m % 2]

        def freed(ins, name, i=None, k=0):
            m, _ = fill(name, i, k)
            return ins.then_inc(acc_free[m % 2], 1)

        def freed_count(name, i=None, k=0):
            m, i = fill(name, i, k)
            return m // 2 + 1 + PER_PAIR // 2 * i

        def last_fill(n, i=0):
            if n < QKV0:
                return fill(f"ada{n}")
            if n < LOOP0:
                return fill("qkvab"[n - QKV0] + "3")
            if n < LOOP0 + 3:
                return fill("pair", i, (0, 6, 5)[n - LOOP0])
            if n < CONV_W:
                return fill("pair", (n - LOOP0) // 3, (0, 6, 5)[(n - LOOP0) % 3])
            if n < OUT_W:
                return fill("cp7" if n == CONV_W else "ap7")
            if n < FIN_W:
                return fill(f"o{4 * (n - OUT_W) + 3}")
            if n < FOUT_W:
                return fill(f"f{4 * (n - FIN_W) + 3}")
            return fill(f"y{n - FOUT_W}")

        def pairs(eng):
            return range(PAIRS)

        def load_pages(eng, ring, cache, full, b, c):
            for g in range(PC * c, PC * c + PC):
                page = eng.value_load(pages[0:1, bass.ds(PG * b + g, 1)], min_val=0, max_val=NPHYS - 1)
                eng.dma_start(ring[:, g, :], cache[bass.ds(page, 1)].rearrange("o p h d -> p (o h d)"))\
                    .then_inc(full[c], 16)

        @block.sync
        def _(sp):
            sp.dma_start(pages[:, :], page_table.rearrange("(o b) p -> o (b p)", o=1)).then_inc(pt_in, 16)
            for t in range(2):
                sp.dma_start(xn[:, t, :], x_prompt[0, t * P:(t + 1) * P, :]).then_inc(x_in, 16)
            sp.dma_start(xn[0:B, 2, :], x_sample[:, 0, :]).then_inc(x_in, 16)

            def load(n, i=0):
                dst = wring[:, n % RING, :]
                if n >= RING:
                    m, ii = last_fill(n, i - 1) if LOOP0 <= n < LOOP0 + 3 and not (isinstance(i, int) and i == 0) \
                        else last_fill(n - RING)
                    sp.wait_ge(acc_full, m + 1 + PER_PAIR * ii)
                full = dst.rearrange("p (k n) -> p k n", k=KD)

                def cols(w, c0, n_):
                    return w[:, c0:c0 + n_].rearrange("(k p) n -> p k n", p=P)

                parts = []
                if n < QKV0:
                    parts = [(full, cols(w_ada, 512 * n, 512))]
                elif n < LOOP0:
                    parts = [(full, cols(w_in, 512 * (n - QKV0), 512))]
                elif n < LOOP0 + 3:
                    r = n - LOOP0
                    if r == 1:
                        parts = [(full, w_in[:, bass.ds(5 * 512 + 512 * i, 512)].rearrange("(k p) n -> p k n", p=P))]
                    else:
                        parts = [(full, w_ada[:, bass.ds(4 * 512 + 1024 * i + 256 * r, 512)]
                                  .rearrange("(k p) n -> p k n", p=P))]
                elif n in (CONV_W, ATTN_W):
                    w = w_conv_proj if n == CONV_W else w_attn_proj
                    parts = [(dst.rearrange("p (k n) -> p k n", k=4), w.rearrange("(k p) n -> p k n", p=P))]
                elif n < FIN_W:
                    parts = [(full, cols(w_out, 512 * (n - OUT_W), 512))]
                elif n < FOUT_W:
                    c0 = 256 * (n - FIN_W)
                    parts = [(full[:, :, 0:256], cols(w_ffn_in, c0, 256)),
                             (full[:, :, 256:512], cols(w_ffn_in, DFF + c0, 256))]
                else:
                    parts = [(dst[:, 0:FT * P].rearrange("p (k n) -> p k n", k=FT),
                              cols(w_ffn_out, P * (n - FOUT_W), P))]
                if len(parts) == 1:
                    (d, s), half = parts[0], parts[0][0].shape[1] // 2
                    parts = [(d[:, 0:half, :], s[:, 0:half, :]), (d[:, half:, :], s[:, half:, :])]
                for d, s in parts:
                    sp.dma_start(d, s).then_inc(w_full[n % RING], 16)

            def load_k(b, c, first=False):
                if not first:
                    sp.wait_ge(k_used, CH * (b - 1) + c + 1)
                load_pages(sp, kring, cache_k, k_full, b, c)

            load(0)
            load(1)
            load(2)
            sp.wait_ge(pt_in, 16)
            load(3)
            load(4)
            load(5)
            for c in range(CH):
                load_k(0, c, first=True)
            load(6)
            load(7)
            load(8)
            load(9)
            load(10)
            for c in range(CH):
                load_k(1, c)
            load(11)
            for i in pairs(sp):
                last = i == PAIRS - 1
                for j in range(2):
                    b = 2 * i + j
                    for c in range(2):
                        if not last:
                            load_k(b + 2, c)
                    if not last:
                        if j == 0:
                            load(LOOP0, i + 1)
                        else:
                            load(LOOP0 + 1, i + 1)
                            load(LOOP0 + 2, i + 1)
                    elif j == 0:
                        load(CONV_W)
                    else:
                        load(ATTN_W)
                        load(OUT_W)
                    for c in range(2, CH):
                        if not last:
                            load_k(b + 2, c)
            for n in range(OUT_W + 1, FOUT_W + KD):
                load(n)
            for t in range(3):
                for e in range(2):
                    sp.wait_ge(acc_free[fill(f"y{t}{e}")[0] % 2], freed_count(f"y{t}{e}"))
                dst = y_prompt[0, t * P:(t + 1) * P, :] if t < 2 else y_sample[:, 0, :]
                sp.dma_start(dst, yn[0:dst.shape[0], t, :]).then_inc(stored, 16)
            sp.wait_ge(stored, 16 * 12)

        @block.gpsimd
        def _(pool):
            steps = [0]

            def step(ins):
                steps[0] += 1
                ins.then_inc(pool_step, 1)
                pool.wait_ge(pool_step, steps[0])

            g = nc.gpsimd
            step(g.memset(ident[:, :], 0.0))
            step(g.affine_select(out=ident[:, :], in_=ident[:, :], compare_op=ALU.not_equal, fill=1.0,
                                 base=0, pattern=[[-1, P]], channel_multiplier=1))
            step(g.memset(ones[:, :], 1.0))
            step(g.memset(halves[:, :], 0.0))
            step(g.memset(eps[:, :], EPS))
            step(g.memset(cT[:, :, :], 0.0))
            step(g.memset(halves[0:DH, 0:DH], 1.0))
            g.memset(halves[DH:P, DH:P], 1.0).then_inc(consts, 1)
            pool.wait_ge(consts, 1)
            step(g.iota(distm[:, 0:P], pattern=[[-1, P]], base=0, channel_multiplier=1,
                        allow_small_or_imprecise_dtypes=True))
            step(g.iota(distm[:, P:384], pattern=[[-1, 2 * P]], base=P, channel_multiplier=1,
                        allow_small_or_imprecise_dtypes=True))
            step(g.affine_select(out=distm[:, 0:P], in_=distm[:, 0:P], compare_op=ALU.is_ge, fill=FAR,
                                 base=0, pattern=[[-1, P]], channel_multiplier=1))
            step(g.affine_select(out=distm[:, P:384], in_=distm[:, P:384], compare_op=ALU.is_ge, fill=FAR,
                                 base=P, pattern=[[-1, 2 * P]], channel_multiplier=1))
            for h in range(H):
                step(g.memset(slopes[:, h:h + 1], -2.0 ** (-8.0 * (h + 1) / H)))
            step(g.iota(dists[:, :], pattern=[[-P, PG]], base=PAST, channel_multiplier=-1,
                        allow_small_or_imprecise_dtypes=True))
            step(g.tensor_tensor(alib[:, :, :], dists[:, :].unsqueeze(2).to_broadcast([P, PG, H]),
                                 slopes[:, :].unsqueeze(1).to_broadcast([P, PG, H]), ALU.mult))
            step(g.memset(lower[:, :, :], 1.0))
            step(g.affine_select(out=lower[:, :, :], in_=lower[:, :, :], compare_op=ALU.is_gt, fill=0.0,
                                 base=0, pattern=[[1, NB], [-1, NB]], channel_multiplier=0))
            step(g.memset(ppad[:, :, :], 0.0))
            step(g.memset(headof[:, :], 0.0))
            for q in range(4):
                step(g.affine_select(out=headof[32 * q:32 * q + 32, :], in_=headof[32 * q:32 * q + 32, :],
                                     compare_op=ALU.not_equal, fill=1.0, base=0, pattern=[[-1, H]],
                                     channel_multiplier=1))
            g.memset(u[:, :, 0:TAPS - 1], 0.0).then_inc(consts, 1)
            pool.wait_ge(consts, 2)

            pool.wait_ge(pt_in, 16)

            def load_v(b):
                if isinstance(b, int) and b == 0:
                    pool.wait_ge(acc_full, fill("st3")[0] + 1)
                for c in range(CH):
                    if not (isinstance(b, int) and b == 0):
                        pool.wait_ge(v_used, CH * (b - 1) + c + 1)
                    load_pages(pool, vring, cache_v, v_full, b, c)

            for b in range(B):
                if b >= 1:
                    pool.wait_ge(gs_ready, b + 1)
                    g.tensor_tensor(sall[:, b % 2, :, :], sall[:, b % 2, :, :], alib[:, :, :], ALU.add)\
                        .then_inc(bias_ready, 1)
                load_v(b)
                if b == 0:
                    pool.wait_ge(gs_ready, b + 1)
                    g.tensor_tensor(sall[:, b % 2, :, :], sall[:, b % 2, :, :], alib[:, :, :], ALU.add)\
                        .then_inc(bias_ready, 1)

        @block.scalar
        def _(act):
            steps = [0]

            def step(ins):
                steps[0] += 1
                ins.then_inc(act_step, 1)
                act.wait_ge(act_step, steps[0])

            def func(out, in_, f, **kw):
                return nc.scalar.activation(out, in_, f, **kw)

            act.dma_start(cn[0:1, :], c_prompt).then_inc(c_in, 16)
            act.dma_start(cn[1:B + 1, :], c_sample).then_inc(c_in, 16)
            for r0, a, n in ((V_ADA, b_ada, 48), (V_G1, g_norm1, 8), (V_G2, g_norm2, 8), (V_BDW, b_dwconv, 4),
                             (V_GLN, g_conv_ln, 4), (V_BLN, b_conv_ln, 4)):
                act.dma_start(vecn[r0:r0 + n, :], a.rearrange("(t p) -> t p", p=P)).then_inc(vec_in, 16)
            for r0, a in ((V_GQ, g_q), (V_GK, g_k)):
                for e in range(2):
                    act.dma_start(vecn[r0:r0 + 1, DH * e:DH * e + DH], a.rearrange("(o d) -> o d", o=1))\
                        .then_inc(vec_in, 16)
            act.dma_start(tapn, w_dwconv.rearrange("t o (c p) -> (t o c) p", p=P)).then_inc(vec_in, 16)
            for t in range(2):
                act.dma_start(stn[:, t, :], state_conv[4 * t:4 * t + 4].rearrange("b t c -> (b t) c")).then_inc(st_in, 16)
            act.dma_start(conv_sample[:, 0:TAPS - 2, :], state_conv[:, 1:TAPS - 1, :]).then_inc(stored, 16)

            act.wait_ge(c_in, 32)
            func(cn, cn, ACT.Silu).then_inc(c_silu, 1)
            bank = when_full(act, "vec")
            freed(func(vt[:, :], bank[:, 0:V_ROWS + TAPS * CT], ACT.Copy), "vec")
            for t in range(KD):
                bank = when_full(act, f"x{t}")
                freed(func(xT[:, t, :], bank[:, 0:R], ACT.Copy), f"x{t}")
            bank = when_full(act, "c")
            freed(func(cT[:, :, 0:B + 1], bank[:, 0:KD * (B + 1)].rearrange("p (k b) -> p k b", k=KD), ACT.Copy), "c")

            def mod_rows(name, i=None, k=0, half=0):
                bank = when_full(act, name, i, k)
                freed(func(mrow[:, half, :], bank[:, 0:P], ACT.Copy), name, i, k)

            n_sq = 0

            def root(name, n, dst):
                bank = when_full(act, name)
                freed(func(dst, bank[:, 0:R], ACT.Sqrt, scale=1.0 / n, bias=eps[:, :]), name)

            root("ss1", D, rstd)
            for n in range(4):
                if n >= 2:
                    act.wait_ge(acc_full, fill(f"adt{n - 2}")[0] + 1)
                mod_rows(f"ada{n}", half=n % 2)

            def raw(name, t):
                nonlocal n_sq
                bank = when_full(act, f"{name}{t}")
                dst = qkvT[:, "qkv".index(name) * 4 + t, :]
                freed(func(dst, bank[:, 0:R], ACT.Copy), f"{name}{t}")
                if name != "v":
                    act.wait_ge(acc_free[fill(f"{name}{t}")[0] % 2], freed_count(f"{name}{t}"))
                    if n_sq >= 4:
                        act.wait_ge(acc_full, fill(f"sqq{n_sq - 4}")[0] + 1)
                    func(tmp2[:, n_sq % 4, :], dst, ACT.Square).then_inc(sq_ready, 1)
                    n_sq += 1

            for t in range(4):
                raw("q", t)
            for t in range(4):
                if t >= 2:
                    act.wait_ge(q_ready, t - 1)
                root(f"sqq{t}", DH, roots[t % 2])
            for t in range(4):
                raw("k", t)
            bank = when_full(act, "qs")
            freed(func(snat[:, :], bank[0:B, :], ACT.Copy), "qs")
            act.wait_ge(acc_free[fill("qs")[0] % 2], freed_count("qs"))

            def select_query(b, first=False):
                if not first:
                    act.wait_ge(qbc_ready, b)
                func(sel[:, :], ident[0:B, bass.ds(b, 1)].to_broadcast([B, P]), ACT.Copy).then_inc(qsel_ready, 1)

            select_query(0, first=True)
            for t in range(4):
                act.wait_ge(*((q_ready, t + 3) if t < 2 else (k_ready, t - 1)))
                root(f"sqk{t}", DH, roots[t % 2])
            for t in range(4):
                raw("v", t)
            for name, dst in (("vn0", vnat[:, 0, :]), ("vn1", vnat[:, 1, :]), ("kn0", knat[:, 0, :]),
                              ("kn1", knat[:, 1, :]), ("ks", skv[:, 0, :]), ("vs", skv[:, 1, :])):
                bank = when_full(act, name)
                freed(func(dst, bank[0:dst.shape[0], :], ACT.Copy), name)
                act.wait_ge(acc_free[fill(name)[0] % 2], freed_count(name))
            for t in range(2):
                act.dma_start(v_prompt[0, t * P:(t + 1) * P].rearrange("p h d -> p (h d)"), vnat[:, t, :]).then_inc(stored, 16)
                act.dma_start(k_prompt[0, t * P:(t + 1) * P].rearrange("p h d -> p (h d)"), knat[:, t, :]).then_inc(stored, 16)
            act.dma_start(k_sample.rearrange("b o h d -> b (o h d)"), skv[:, 0, :]).then_inc(stored, 16)
            act.dma_start(v_sample.rearrange("b o h d -> b (o h d)"), skv[:, 1, :]).then_inc(stored, 16)
            bank = when_full(act, "so")
            freed(func(sown[:, :, :].rearrange("p b h -> p (b h)"), bank[:, 0:B * H], ACT.Copy), "so")
            for t in range(4):
                bank = when_full(act, f"a{t}")
                freed(func(u[:, t, TAPS - 1:], bank[:, 0:R], ACT.Copy), f"a{t}")
            for t in range(4):
                bank = when_full(act, f"b{t}")
                freed(func(tmp2[:, t, :], bank[:, 0:R], ACT.Sigmoid), f"b{t}")
            bank = when_full(act, "ct")
            freed(func(ctn[:, :], bank[0:TAPS - 1 + B, :], ACT.Copy), "ct")
            act.wait_ge(acc_free[fill("ct")[0] % 2], freed_count("ct"))
            act.dma_start(conv_prompt[0], ctn[0:TAPS - 1, :]).then_inc(stored, 16)
            act.dma_start(conv_sample[:, TAPS - 2, :], ctn[TAPS - 1:, :]).then_inc(stored, 16)
            act.wait_ge(stored, 16 * 9)
            act.wait_ge(k_ready, 4)

            for i in pairs(act):
                for j in range(2):
                    b = 2 * i + j
                    last = i == PAIRS - 1 and j == 1
                    if not last:
                        select_query(b + 1)
                    if j == 0:
                        if not (isinstance(i, int) and i == 0):
                            act.wait_ge(pp_ready, b)
                        act.wait_ge(ps_ready, b)
                        func(qst[:, :], qT[:, bass.ds(i, 1), 0:S].rearrange("p o n -> p (o n)"), ACT.Copy).then_inc(st_ready, 1)
                        func(kst[:, :], kT[:, bass.ds(i, 1), 0:S].rearrange("p o n -> p (o n)"), ACT.Copy).then_inc(st_ready, 1)
                        func(vst[:, :, :], vnat[:, :, bass.ds(P * i, P)], ACT.Copy).then_inc(st_ready, 1)
                    act.wait_ge(pb_ready, b + 1)
                    for t, (c0, c1) in enumerate(((0, P), (P, 384))):
                        func(pr[:, c0:c1], pr[:, c0:c1], ACT.Exp, bias=pmx[:, t:t + 1],
                             accum_out=psum_[:, t:t + 1]).then_inc(pe_ready, 1)
                    act.wait_ge(pt_ready, b + 1)
                    act.wait_ge(pp_ready, b)
                    func(prT[:, :], psT[:, 0:384], ACT.Copy).then_inc(pc_ready, 1)
                    for k in range(4 * j, 4 * j + 4):
                        if PAIR[k][:3] == "ada":
                            mod_rows("pair", i, k, half=j)
                        elif PAIR[k][0] == "g":
                            bank = when_full(act, "pair", i, k)
                            freed(func(gates[:, bass.ds(4 * i + int(PAIR[k][1]), 1), :].rearrange("p o n -> p (o n)"),
                                       bank[:, 0:R], ACT.Sigmoid), "pair", i, k)
                    act.wait_ge(s2_ready, b + 1)
                    func(s1[:, :, :], s1[:, :, :], ACT.Exp).then_inc(e_ready, 1)
                    act.wait_ge(pp_ready, b + 1)
                    func(oT[DH * j:DH * j + DH, bass.ds(i, 1), 0:S].rearrange("p o n -> p (o n)"),
                         psO[DH * j:DH * j + DH, 0:S], ACT.Copy).then_inc(po_ready, 1)

            root("lnv", C, rstd)
            act.wait_ge(ln_s, 1)
            for t in range(CT):
                func(cvT[:, t, :], cvT[:, t, :], ACT.Silu, scale=vec[:, V_GLN + t:V_GLN + t + 1],
                     bias=vec[:, V_BLN + t:V_BLN + t + 1]).then_inc(cv_ready, 1)
            root("ss2", D, rstd)
            for n in range(FT):
                bank = when_full(act, f"f{2 * n}")
                if n >= 2:
                    act.wait_ge(acc_free[fill(f"f{2 * n - 3}")[0] % 2], freed_count(f"f{2 * n - 3}"))
                freed(func(tmp2[:, n % 2, :], bank[:, 0:R], ACT.Silu), f"f{2 * n}")
            for t in range(3):
                rows = P if t < 2 else B
                for e in range(2):
                    bank = when_full(act, f"y{t}{e}")
                    freed(func(yn[0:rows, t, 512 * e:512 * e + 512], bank[0:rows, :], ACT.Copy), f"y{t}{e}")

        @block.vector
        def _(dve):
            v = nc.vector
            steps = [0]

            def step(ins):
                steps[0] += 1
                ins.then_inc(dve_step, 1)
                dve.wait_ge(dve_step, steps[0])

            def wide(ap, shape):
                return ap.to_broadcast(shape)

            dve.wait_ge(acc_free[fill("vec")[0] % 2], freed_count("vec"))
            for t in range(CT):
                bank = when_full(dve, f"st{t}")
                w = taps[:, 0:TAPS - 1, t].unsqueeze(1).to_broadcast([P, B, TAPS - 1])
                scr = cvT[:, 0, 0:B * (TAPS - 1)].rearrange("p (b t) -> p b t", b=B)
                ins = v.tensor_tensor(scr, bank[:, 0:B * (TAPS - 1)].rearrange("p (b t) -> p b t", b=B), w, ALU.mult)
                freed(ins, f"st{t}")
                dve.wait_ge(acc_free[fill(f"st{t}")[0] % 2], freed_count(f"st{t}"))
                step(v.tensor_reduce(cvs[:, t, :], scr, AX.X, ALU.add))
            dve.wait_ge(acc_free[fill("x7")[0] % 2], freed_count("x7"))
            dve.wait_ge(acc_free[fill("x6")[0] % 2], freed_count("x6"))
            v.tensor_tensor(hT[:, :, :], xT[:, :, :], xT[:, :, :], ALU.mult).then_inc(x_sq, 1)
            step(v.tensor_scalar(vec[:, V_GQ:V_GQ + 1], vec[:, V_GQ:V_GQ + 1], DH ** -0.5, None, ALU.mult))

            def row_factors(name):
                dve.wait_ge(acc_free[fill(name)[0] % 2], freed_count(name))
                step(v.reciprocal(rstd, rstd))

            def modulation(slot, name, i=None, k=0):
                bank = when_full(dve, name, i, k)
                ins = v.tensor_tensor(modT[:, bass.ds(4 * slot, 4), :],
                                      bank[:, 0:P].rearrange("p (t b) -> p t b", t=4)[:, :, 0:B + 1],
                                      vec[:, bass.ds(V_ADA + 4 * slot, 4)].unsqueeze(2).to_broadcast([P, 4, B + 1]),
                                      ALU.add)
                freed(ins, name, i, k)
                dve.wait_ge(acc_free[fill(name, i, k)[0] % 2], freed_count(name, i, k))

            def norm(g_row, shift, scale, src, out_sem):
                step(v.tensor_scalar(gs[:, :, :], modT[:, scale:scale + KD, :], 1.0, None, ALU.add))
                step(v.tensor_tensor(gs[:, :, :], gs[:, :, :],
                                     vec[:, g_row:g_row + KD].unsqueeze(2).to_broadcast([P, KD, B + 1]), ALU.mult))
                step(v.tensor_tensor(hT[:, :, :], src, rstd[:, :].unsqueeze(1).to_broadcast([P, KD, R]), ALU.mult))
                step(v.tensor_tensor(hT[:, :, S:R], hT[:, :, S:R], gs[:, :, 1:B + 1], ALU.mult))
                step(v.tensor_tensor(hT[:, :, S:R], hT[:, :, S:R], modT[:, shift:shift + KD, 1:B + 1], ALU.add))
                for t in range(KD):
                    v.tensor_scalar(hT[:, t, 0:S], hT[:, t, 0:S], gs[:, t, 0:1], modT[:, shift + t, 0:1],
                                    ALU.mult, ALU.add).then_inc(out_sem, 1)

            row_factors("ss1")
            for n in range(4):
                modulation(n, f"adt{n}")
            norm(V_G1, 0, 8, xT[:, :, :], h_ready)

            def head_norm(name, t):
                dve.wait_ge(acc_free[fill(f"sq{name}{t}")[0] % 2], freed_count(f"sq{name}{t}"))
                root = roots[t % 2]
                step(v.reciprocal(root, root))
                tile = qkvT[:, "qk".index(name) * 4 + t, :]
                g = V_GQ if name == "q" else V_GK
                v.scalar_tensor_tensor(tile, tile, vec[:, g:g + 1], root, ALU.mult, ALU.mult)\
                    .then_inc(q_ready if name == "q" else k_ready, 1)

            for t in range(4):
                head_norm("q", t)
                dve.wait_ge(q_ready, t + 1)
            for t in range(4):
                head_norm("k", t)
                dve.wait_ge(k_ready, t + 1)

            def score(b, j, c):
                dve.wait_ge(k_full[c], 16 * PC * (b + 1))
                if c == 0:
                    dve.wait_ge(qbc_ready, b + 1)
                hp = PC // 2
                for e in range(2):
                    g0 = PC * c + hp * e
                    ins = v.tensor_tensor(prod[:, :, :], kring[:, g0:g0 + hp, :],
                                          qbc[j][:, :].unsqueeze(1).to_broadcast([P, hp, A]), ALU.mult)
                    if e == 0:
                        step(ins)
                    else:
                        ins.then_inc(k_used, 1)
                        dve.wait_ge(k_used, CH * b + c + 1)
                    ins = v.tensor_reduce(sall[:, j, g0:g0 + hp, :].rearrange("p g h -> p (g h)"),
                                          prod[:, :, :].rearrange("p g (h d) -> p (g h) d", d=DH), AX.X, ALU.add)
                    if e == 0:
                        step(ins)
                    else:
                        ins.then_inc(scored, 1)
                        dve.wait_ge(scored, CH * b + c + 1)

            score(0, 0, 0)
            score(0, 0, 1)
            dve.wait_ge(acc_free[fill("ks")[0] % 2], freed_count("ks"))
            step(v.tensor_tensor(ownp, snat[:, :], skv[:, 0, :], ALU.mult))
            step(v.tensor_reduce(soq[:, 0, 0:H], ownp.rearrange("p (h d) -> p h d", d=DH), AX.X, ALU.add))
            v.tensor_tensor(soq[:, 1, :].rearrange("p (b h) -> p b h", b=B),
                            soq[:, 0, 0:H].unsqueeze(1).to_broadcast([B, B, H]),
                            ident[0:B, 0:B].unsqueeze(2).to_broadcast([B, B, H]), ALU.mult).then_inc(so_ready, 1)
            score(0, 0, 2)
            score(0, 0, 3)
            for t in range(4):
                dve.wait_ge(acc_free[fill(f"b{t}")[0] % 2], freed_count(f"b{t}"))
                v.tensor_tensor(u[:, t, TAPS - 1:], u[:, t, TAPS - 1:], tmp2[:, t, :], ALU.mult).then_inc(u_ready, 1)
                dve.wait_ge(u_ready, t + 1)

            dve.wait_ge(consts, 2)
            for i in pairs(dve):
                for j in range(2):
                    b = 2 * i + j
                    last = i == PAIRS - 1 and j == 1
                    if not last:
                        score(b + 1, 1 - j, 0)
                    dve.wait_ge(gs_ready, b + 1)
                    idh = ident[0:H, 0:H].unsqueeze(1)
                    step(v.tensor_tensor(diag[:, :, :], chain[0:H, 0:PG * H].rearrange("p (g h) -> p g h", h=H),
                                         idh.to_broadcast([H, PG, H]), ALU.mult))
                    step(v.tensor_reduce(gate[:, :], diag[:, :, :].rearrange("p (n e) h -> p n (e h)", e=2),
                                         AX.X, ALU.add))
                    gm = gate[:, :].unsqueeze(1).to_broadcast([H, NB, NB])
                    gn = gate[:, :].unsqueeze(2).to_broadcast([H, NB, NB])
                    step(v.tensor_tensor(cmp1[:, :, :], gm, gn, ALU.is_equal))
                    step(v.tensor_tensor(cmp1[:, :, :], cmp1[:, :, :], lower[0:H, :, :], ALU.mult))
                    step(v.tensor_tensor(cmp2[:, :, :], gm, gn, ALU.is_gt))
                    step(v.tensor_tensor(cmp1[:, :, :], cmp1[:, :, :], cmp2[:, :, :], ALU.add))
                    step(v.tensor_reduce(gate[:, :], cmp1[:, :, :], AX.X, ALU.add))
                    step(v.tensor_scalar(gate[:, :], gate[:, :], float(TOPK), NEG, ALU.is_ge, ALU.mult))
                    v.tensor_tensor(cmp2[:, :, :], gate[:, :].unsqueeze(2).to_broadcast([H, NB, H]),
                                    idh.to_broadcast([H, NB, H]), ALU.mult).then_inc(pen_ready, 1)
                    dve.wait_ge(ps_ready, b + 1)
                    dve.wait_ge(pt_ready, b)
                    step(v.scalar_tensor_tensor(pr[:, :], distm[:, :], slopes[:, bass.ds(b, 1)], psS[:, 0:384],
                                                ALU.mult, ALU.add))
                    step(v.tensor_reduce(pmx[:, 0:1], pr[:, 0:P], AX.X, ALU.max, negate=True))
                    v.tensor_reduce(pmx[:, 1:2], pr[:, P:384], AX.X, ALU.max, negate=True).then_inc(pb_ready, 1)
                    dve.wait_ge(mask_ready, b + 1)
                    dve.wait_ge(bias_ready, b + 1)
                    step(v.tensor_tensor(s1[:, 0:PG, :].rearrange("p (n e) h -> p n e h", e=2),
                                         sall[:, j, :, :].rearrange("p (n e) h -> p n e h", e=2),
                                         chain[:, 0:NB * H].rearrange("p (n h) -> p n h", h=H).unsqueeze(2)
                                         .to_broadcast([P, NB, 2, H]), ALU.add))
                    step(v.tensor_copy(s1[:, PG, :], sown[:, bass.ds(b, 1), :].rearrange("p o h -> p (o h)")))
                    v.tensor_reduce(m1, s1[:, :, :].rearrange("p g h -> p h g"), AX.X, ALU.max).then_inc(m1_ready, 1)
                    if not last:
                        score(b + 1, 1 - j, 1)
                    dve.wait_ge(pe_ready, 2 * b + 2)
                    step(v.reciprocal(prin, psum_))
                    step(v.tensor_scalar(pr[:, 0:P], pr[:, 0:P], prin[:, 0:1], None, ALU.mult))
                    v.tensor_scalar(pr[:, P:384], pr[:, P:384], prin[:, 1:2], None, ALU.mult).then_inc(pn_ready, 1)
                    dve.wait_ge(m1t_ready, b + 1)
                    step(v.tensor_reduce(nmx, chain[0:H, 0:P], AX.X, ALU.max, negate=True))
                    v.tensor_scalar(dg, ident[0:H, 0:H], nmx, None, ALU.mult).then_inc(dg_ready, 1)
                    if j == 0:
                        modulation(4 + 2 * i, "pair", i, 2)
                    dve.wait_ge(mb_ready, b + 1)
                    v.tensor_tensor(s1[:, :, :], s1[:, :, :], chain[:, 0:H].unsqueeze(1).to_broadcast([P, PG + 1, H]),
                                    ALU.add).then_inc(s2_ready, 1)
                    if not last:
                        score(b + 1, 1 - j, 2)
                    dve.wait_ge(e_ready, b + 1)
                    v.tensor_reduce(es, s1[:, 0:PG, :].rearrange("p g h -> p h g"), AX.X, ALU.add).then_inc(es_ready, 1)
                    if not last:
                        score(b + 1, 1 - j, 3)
                    dve.wait_ge(tot_ready, b + 1)
                    step(v.tensor_tensor(rinv, chain[:, 0:H], s1[:, PG, :], ALU.add))
                    step(v.reciprocal(rinv, rinv))
                    v.tensor_tensor(ppad[:, :, 0:H], s1[:, 0:PG, :], rinv.unsqueeze(1).to_broadcast([P, PG, H]),
                                    ALU.mult).then_inc(p_ready, 1)
                    step(v.tensor_tensor(s1[:, PG, :], s1[:, PG, :], rinv, ALU.mult))
                    if j == 1:
                        modulation(5 + 2 * i, "pair", i, 7)
                    cv = cvT[:, bass.ds(i, 1), 0:S].rearrange("p o n -> p (o n)")
                    for tap in (range(0, 16) if j == 0 else range(16, TAPS)):
                        src = u[:, bass.ds(i, 1), tap:tap + S].rearrange("p o n -> p (o n)")
                        w = taps[:, tap, bass.ds(i, 1)]
                        if tap == 0:
                            step(v.tensor_scalar(cv, src, w, vec[:, bass.ds(V_BDW + i, 1)], ALU.mult, ALU.add))
                        else:
                            step(v.scalar_tensor_tensor(cv, src, w, cv, ALU.mult, ALU.add))
                    for e in range(2):
                        rows = slice(DH * e, DH * e + DH)
                        step(v.tensor_tensor(own[rows, :], s1[rows, PG, e:H:2],
                                             vT[rows, :, bass.ds(S + b, 1)].rearrange("p t o -> p (t o)"), ALU.mult))
                    dve.wait_ge(v_used, CH * (b + 1))
                    v.tensor_tensor(pvm[:, :].rearrange("p (h d) -> p h d", d=DH),
                                    chain[:, :].rearrange("p (h d) -> p h d", d=DH),
                                    headof[:, :].unsqueeze(2).to_broadcast([P, H, DH]), ALU.mult).then_inc(pvm_ready, 1)
                    dve.wait_ge(pv_ready, b + 1)
                    for e in range(2):
                        rows = slice(DH * e, DH * e + DH)
                        v.tensor_tensor(oT[rows, :, bass.ds(S + b, 1)].rearrange("p t o -> p (t o)"), own[rows, :],
                                        chain[rows, 0:AT], ALU.add).then_inc(o_ready, 1)
                    dve.wait_ge(o_ready, 2 * b + 2)

            w30 = taps[:, TAPS - 1, :].unsqueeze(2).to_broadcast([P, CT, B])
            step(v.tensor_tensor(cvs[:, :, :], cvs[:, :, :],
                                 vec[:, V_BDW:V_BDW + CT].unsqueeze(2).to_broadcast([P, CT, B]), ALU.add))
            step(v.tensor_tensor(cvT[:, :, S:R], u[:, :, TAPS - 1 + S:], w30, ALU.mult))
            v.tensor_tensor(cvT[:, :, S:R], cvT[:, :, S:R], cvs[:, :, :], ALU.add).then_inc(ln_c, 1)
            bank = when_full(dve, "lnm")
            freed(v.tensor_scalar(rstd[:, :], bank[:, 0:R], 1.0 / C, None, ALU.mult), "lnm")
            dve.wait_ge(acc_free[fill("lnm")[0] % 2], freed_count("lnm"))
            step(v.tensor_tensor(cvT[:, :, :], cvT[:, :, :], rstd[:, :].unsqueeze(1).to_broadcast([P, CT, R]), ALU.subtract))
            v.tensor_tensor(qkvT[:, 0:4, :], cvT[:, :, :], cvT[:, :, :], ALU.mult).then_inc(ln_c, 1)
            row_factors("lnv")
            v.tensor_tensor(cvT[:, :, :], cvT[:, :, :], rstd[:, :].unsqueeze(1).to_broadcast([P, CT, R]), ALU.mult)\
                .then_inc(ln_s, 1)
            dve.wait_ge(acc_free[fill("pair", 0, 4)[0] % 2], freed_count("pair", PAIRS - 1, 4))
            dve.wait_ge(acc_free[fill("pair", 0, 6)[0] % 2], freed_count("pair", PAIRS - 1, 6))
            dve.wait_ge(acc_free[fill("pair", 0, 3)[0] % 2], freed_count("pair", PAIRS - 1, 3))
            for t in range(8):
                bank = when_full(dve, f"cp{t}")
                freed(v.tensor_tensor(hT[:, t, :], bank[:, 0:R], gates[:, 8 + t, :], ALU.mult), f"cp{t}")
            for t in range(8):
                bank = when_full(dve, f"ap{t}")
                freed(v.tensor_tensor(qkvT[:, 4 + t % 2, :], bank[:, 0:R], gates[:, t, :], ALU.mult), f"ap{t}")
                dve.wait_ge(acc_free[fill(f"ap{t}")[0] % 2], freed_count(f"ap{t}"))
                v.tensor_tensor(hT[:, t, :], hT[:, t, :], qkvT[:, 4 + t % 2, :], ALU.add).then_inc(mix_ready, 1)

            def gated_add(name, gt, t, out_sem):
                bank = when_full(dve, name)
                step(v.tensor_tensor(cvs[:, 0, :], bank[:, S:R], modT[:, gt + t, 1:B + 1], ALU.mult))
                freed(v.scalar_tensor_tensor(xT[:, t, 0:S], bank[:, 0:S], modT[:, gt + t, 0:1], xT[:, t, 0:S],
                                             ALU.mult, ALU.add), name)
                v.tensor_tensor(xT[:, t, S:R], xT[:, t, S:R], cvs[:, 0, :], ALU.add).then_inc(out_sem, 1)

            for t in range(8):
                gated_add(f"o{t}", 16, t, x2_ready)
                dve.wait_ge(x2_ready, t + 1)
                dve.wait_ge(acc_free[fill(f"o{t}")[0] % 2], freed_count(f"o{t}"))
                v.tensor_tensor(sq[:, t, :], xT[:, t, :], xT[:, t, :], ALU.mult).then_inc(x2_sq, 1)
            row_factors("ss2")
            norm(V_G2, 24, 32, xT[:, :, :], h2_ready)
            for n in range(FT):
                bank = when_full(dve, f"f{2 * n + 1}")
                m = fill(f"f{2 * n}")
                dve.wait_ge(acc_free[m[0] % 2], freed_count(f"f{2 * n}"))
                freed(v.tensor_tensor(fT[:, n, :], bank[:, 0:R], tmp2[:, n % 2, :], ALU.mult), f"f{2 * n + 1}")
                dve.wait_ge(acc_free[fill(f"f{2 * n + 1}")[0] % 2], freed_count(f"f{2 * n + 1}"))
            for t in range(8):
                gated_add(f"y{t}", 40, t, y_ready)
                dve.wait_ge(y_ready, t + 1)

        @block.tensor
        def _(pe):
            mm = nc.tensor.matmul

            def bank_for(name, i=None, k=0):
                m, ii = fill(name, i, k)
                if not (isinstance(ii, int) and m + PER_PAIR * ii < 2):
                    pe.wait_ge(acc_free[m % 2], m // 2 + PER_PAIR // 2 * ii)
                return acc[m % 2]

            def slot_ready(n, i=0):
                pe.wait_ge(w_full[n % RING], 32 * (n // RING + 1 + i))
                return wring[:, n % RING, :]

            def product(bank, c0, width, w, tile, src, last_inc=None, cols=None):
                nk = w.shape[1]
                for k in range(nk):
                    ins = mm(bank[:, c0:c0 + width], w[:, k, P * tile:P * tile + P], src[:, k, :],
                             start=k == 0, stop=k == nk - 1)
                return ins

            pe.wait_ge(consts, 1)
            pe.wait_ge(vec_in, 16 * 11)
            bank = bank_for("vec")
            nc.tensor.transpose(bank[:, 0:V_ROWS], vecn, ident[0:V_ROWS, 0:V_ROWS])
            nc.tensor.transpose(bank[:, V_ROWS:V_ROWS + TAPS * CT], tapn, ident[0:TAPS * CT, 0:TAPS * CT]).then_inc(acc_full, 1)
            pe.wait_ge(x_in, 48)
            for t in range(KD):
                bank = bank_for(f"x{t}")
                for r in range(2):
                    nc.tensor.transpose(bank[:, P * r:P * r + P], xn[:, r, P * t:P * t + P], ident[:, :])
                nc.tensor.transpose(bank[:, S:R], xn[0:B, 2, P * t:P * t + P], ident[0:B, 0:B]).then_inc(acc_full, 1)
            pe.wait_ge(c_silu, 1)
            bank = bank_for("c")
            n9 = B + 1
            for t in range(KD):
                ins = nc.tensor.transpose(bank[:, n9 * t:n9 * t + n9], cn[:, P * t:P * t + P], ident[0:n9, 0:n9])
            ins.then_inc(acc_full, 1)
            pe.wait_ge(st_in, 32)
            for t in range(CT):
                bank = bank_for(f"st{t}")
                for r in range(2):
                    ins = nc.tensor.transpose(bank[:, 120 * r:120 * r + 120], stn[:, r, P * t:P * t + P], ident[0:120, 0:120])
                ins.then_inc(acc_full, 1)
            def sums(name, src, nk, lhsT=ones, done=None):
                bank = bank_for(name)
                for k in range(nk):
                    ins = mm(bank[:, 0:R], lhsT[:, :], src[:, k, :], start=k == 0, stop=k == nk - 1)
                ins.then_inc(acc_full, 1)

            pe.wait_ge(x_sq, 1)
            sums("ss1", hT, KD)

            def modulation(n, i, name, k=0):
                w = slot_ready(n, i).rearrange("p (k n) -> p k n", k=KD)
                bank = bank_for(name, i, k)
                for kk in range(KD):
                    for t in range(4):
                        ins = mm(bank[32 * t:32 * t + 32, 0:P], cT[:, kk, :], w[:, kk, P * t:P * t + P],
                                 start=kk == 0, stop=kk == KD - 1)
                ins.then_inc(acc_full, 1)

            def mod_turned(src, i, name, k=0, half=0):
                m, ii = fill(src[0], i, src[1])
                pe.wait_ge(acc_free[m % 2], m // 2 + 1 + PER_PAIR // 2 * ii)
                bank = bank_for(name, i, k)
                nc.tensor.transpose(bank[:, 0:P], mrow[:, half, :], ident[:, :]).then_inc(acc_full, 1)

            pe.wait_ge(acc_free[fill("c")[0] % 2], freed_count("c"))
            for n in range(5):
                if n < 4:
                    modulation(ADA0 + n, 0, f"ada{n}")
                if n >= 1:
                    mod_turned((f"ada{n - 1}", 0), 0, f"adt{n - 1}", half=(n - 1) % 2)

            def rows(n, names, src, tiles=None, ready=None):
                w = slot_ready(n).rearrange("p (k n) -> p k n", k=KD)
                for t, name in zip(tiles or range(len(names)), names):
                    bank = bank_for(name)
                    for k in range(KD):
                        if ready is not None and name == names[0]:
                            pe.wait_ge(ready, k + 1)
                        ins = mm(bank[:, 0:R], w[:, k, P * t:P * t + P], src[:, k, :], start=k == 0, stop=k == KD - 1)
                    ins.then_inc(acc_full, 1)

            def to_rows(name, src, c0, n, wait=None):
                bank = bank_for(name)
                for t in range(4):
                    ins = nc.tensor.transpose(bank[0:n, P * t:P * t + P], src[:, t, c0:c0 + n], ident[:, :])
                ins.then_inc(acc_full, 1)

            def spread_query(b, j, first=False):
                pe.wait_ge(qsel_ready, b + 1)
                if not first:
                    pe.wait_ge(k_used, CH * (b - 1))
                mm(qbc[j][:, :], sel[:, :], snat[:, :], start=True, stop=True).then_inc(qbc_ready, 1)

            rows(QKV0, [f"q{t}" for t in range(4)], hT, ready=h_ready)
            for t in range(4):
                pe.wait_ge(sq_ready, t + 1)
                sums(f"sqq{t}", tmp2[:, t:t + 1, :], 1, halves)
            rows(QKV0 + 1, [f"k{t}" for t in range(4)], hT)
            pe.wait_ge(q_ready, 4)
            to_rows("qs", qT, S, B)
            for t in range(4):
                pe.wait_ge(sq_ready, t + 5)
                sums(f"sqk{t}", tmp2[:, t:t + 1, :], 1, halves)
            spread_query(0, 0, first=True)
            rows(QKV0 + 2, [f"v{t}" for t in range(4)], hT)
            pe.wait_ge(acc_free[fill("v2")[0] % 2], freed_count("v2"))
            pe.wait_ge(acc_free[fill("v3")[0] % 2], freed_count("v3"))
            to_rows("vn0", vT, 0, P)
            to_rows("vn1", vT, P, P)
            pe.wait_ge(k_ready, 4)
            to_rows("kn0", kT, 0, P)
            to_rows("kn1", kT, P, P)
            to_rows("ks", kT, S, B)
            to_rows("vs", vT, S, B)
            pe.wait_ge(so_ready, 1)
            bank = bank_for("so")
            mm(bank[:, 0:B * H], ones[0:B, :], soq[:, 1, :], start=True, stop=True).then_inc(acc_full, 1)
            rows(GLU0, [f"a{t}" for t in range(4)], hT)
            rows(GLU0 + 1, [f"b{t}" for t in range(4)], hT)
            pe.wait_ge(u_ready, 4)
            to_rows("ct", u, S, TAPS - 1 + B)

            for i in pairs(pe):
                for j in range(2):
                    b = 2 * i + j
                    last = i == PAIRS - 1 and j == 1
                    if not last:
                        spread_query(b + 1, 1 - j)
                    pe.wait_ge(scored, CH * (b + 1))
                    pe.wait_ge(o_ready, 2 * b)
                    mm(chain[0:H, 0:PG * H], ones[:, 0:H], sall[:, j, :, :].rearrange("p g h -> p (g h)"),
                       start=True, stop=True).then_inc(gs_ready, 1)
                    rws = slice(DH * j, DH * j + DH)
                    pe.wait_ge(st_ready, 3 * i + 2)
                    pe.wait_ge(pb_ready, b)
                    mm(psS[:, 0:P], qst[rws, 0:P], kst[rws, 0:P], start=True, stop=True)
                    mm(psS[:, P:384], qst[rws, P:S], kst[rws, :], start=True, stop=True).then_inc(ps_ready, 1)
                    pe.wait_ge(pen_ready, b + 1)
                    mm(chain[:, 0:NB * H], ones[0:H, :], cmp2[:, :, :].rearrange("p n h -> p (n h)"),
                       start=True, stop=True).then_inc(mask_ready, 1)
                    pe.wait_ge(m1_ready, b + 1)
                    nc.tensor.transpose(chain[0:H, 0:P], m1, ident[:, :]).then_inc(m1t_ready, 1)
                    pe.wait_ge(pn_ready, b + 1)
                    pe.wait_ge(pc_ready, b)
                    for t in range(3):
                        ins = nc.tensor.transpose(psT[:, P * t:P * t + P], pr[:, P * t:P * t + P], ident[:, :])
                    ins.then_inc(pt_ready, 1)
                    w = slot_ready(LOOP0 + 1, i).rearrange("p (k n) -> p k n", k=KD)
                    for k in range(4 * j, 4 * j + 4):
                        if PAIR[k][0] == "g":
                            product(bank_for("pair", i, k), 0, R, w, int(PAIR[k][1]), hT).then_inc(acc_full, 1)
                        elif PAIR[k][:3] == "ada":
                            modulation(LOOP0 + 2 * j, i, "pair", k)
                        else:
                            mod_turned(("pair", k - 2), i, "pair", k, half=j)
                        if k % 4 == 1:
                            pe.wait_ge(dg_ready, b + 1)
                            mm(chain[:, 0:H], ones[0:H, :], dg, start=True, stop=True).then_inc(mb_ready, 1)
                            pe.wait_ge(pc_ready, b + 1)
                            pe.wait_ge(st_ready, 3 * i + 3)
                            pe.wait_ge(po_ready, b)
                            mm(psO[rws, 0:S], vst[:, 0, rws], prT[:, 0:S], start=True, stop=False)
                            mm(psO[rws, P:S], vst[:, 1, rws], prT[:, S:384], start=False, stop=True).then_inc(pp_ready, 1)
                    pe.wait_ge(es_ready, b + 1)
                    mm(chain[:, 0:H], ones[:, :], es, start=True, stop=True).then_inc(tot_ready, 1)
                    pe.wait_ge(p_ready, b + 1)
                    for c in range(CH):
                        pe.wait_ge(v_full[c], 16 * PC * (b + 1))
                        for q in range(PC):
                            ins = mm(chain[32 * q:32 * q + 32, :], ppad[:, PC * c + q, :], vring[:, PC * c + q, :],
                                     start=c == 0, stop=c == CH - 1)
                        ins.then_inc(v_used, 1)
                    pe.wait_ge(pvm_ready, b + 1)
                    for t in range(AT):
                        ins = mm(chain[:, t:t + 1], pvm[:, P * t:P * t + P], ones[:, 0:1], start=True, stop=True)
                    ins.then_inc(pv_ready, 1)

            pe.wait_ge(ln_c, 1)
            sums("lnm", cvT, CT)
            pe.wait_ge(ln_c, 2)
            sums("lnv", qkvT, CT)
            for n, name, src in ((CONV_W, "cp", cvT), (ATTN_W, "ap", oT)):
                w = slot_ready(n).rearrange("p (k n) -> p k n", k=4)
                if name == "cp":
                    pe.wait_ge(cv_ready, CT)
                else:
                    pe.wait_ge(o_ready, 2 * B)
                    pe.wait_ge(po_ready, B)
                for t in range(8):
                    product(bank_for(f"{name}{t}"), 0, R, w, t, src).then_inc(acc_full, 1)
            rows(OUT_W, [f"o{t}" for t in range(4)], hT, ready=mix_ready)
            rows(OUT_W + 1, [f"o{t}" for t in range(4, 8)], hT)
            pe.wait_ge(x2_sq, KD)
            sums("ss2", sq, KD)
            for n in range(FT // 2):
                rows(FIN_W + n, [f"f{4 * n + e}" for e in range(4)], hT, tiles=(0, 2, 1, 3),
                     ready=h2_ready if n == 0 else None)
            pe.wait_ge(acc_free[fill(f"f{2 * FT - 1}")[0] % 2], freed_count(f"f{2 * FT - 1}"))
            for t in range(8):
                w = slot_ready(FOUT_W + t)[:, 0:FT * P].rearrange("p (k n) -> p k n", k=FT)
                product(bank_for(f"y{t}"), 0, R, w, 0, fT).then_inc(acc_full, 1)
            for t in range(3):
                n = P if t < 2 else B
                for e in range(2):
                    pe.wait_ge(y_ready, 8)
                    to_rows(f"y{t}{e}", xT[:, 4 * e:4 * e + 4, :], P * t, n)


INS = ["x_prompt", "x_sample", "cache_k", "cache_v", "state_conv", "page_table", "c_prompt", "c_sample",
       "w_ada", "b_ada", "g_norm1", "w_in", "g_q", "g_k", "w_attn_proj", "w_dwconv", "b_dwconv",
       "g_conv_ln", "b_conv_ln", "w_conv_proj", "w_out", "g_norm2", "w_ffn_in", "w_ffn_out"]
OUTS = [("y_prompt", (1, S, D)), ("y_sample", (B, 1, D)), ("k_prompt", (1, S, H, DH)), ("v_prompt", (1, S, H, DH)),
        ("conv_prompt", (1, TAPS - 1, C)), ("k_sample", (B, 1, H, DH)), ("v_sample", (B, 1, H, DH)),
        ("conv_sample", (B, TAPS - 1, C))]


def kernel(**inputs):
    import numpy as np
    import concourse.bacc as bacc
    from concourse.bass_utils import run_bass_kernel_spmd

    nc = bacc.Bacc("TRN2", target_bir_lowering=False, num_devices=1)
    arrays, args = {}, {}
    for name in INS:
        a = np.ascontiguousarray(inputs[name])
        arrays[f"in_{name}"] = a
        args[name] = nc.dram_tensor(f"in_{name}", a.shape, mybir.dt.from_np(a.dtype), kind="ExternalInput").ap()
    for name, shape in OUTS:
        args[name] = nc.dram_tensor(f"out_{name}", shape, F32, kind="ExternalOutput").ap()
    program(nc, **args)
    r = run_bass_kernel_spmd(nc, [arrays], core_ids=[0])
    return tuple(r.results[0][f"out_{name}"] for name, _ in OUTS)
```

```python
from contextlib import ExitStack

import concourse.bass as bass
from concourse import mybir

F32 = mybir.dt.float32
I32 = mybir.dt.int32
ALU = mybir.AluOpType
ACT = mybir.ActivationFunctionType
AX = mybir.AxisListType

P = 128
D = 1024
KD = D // P
S = 256
B = 8
R = S + B
H, DH = 8, 64
A = H * DH
AT = A // P
C = 512
CT = C // P
TAPS = 31
DFF = 2816
FT = DFF // P
PG = 16
CH = 4
PC = PG // CH
NB = 8
TOPK = 3
PAST = PG * P
NPHYS = 160
EPS = 1e-6
NEG = -1e30
FAR = 1e33
SLOT = 4096
RING = 3
PAIRS = B // 2

V_ADA, V_G1, V_G2, V_BDW, V_GLN, V_BLN, V_GQ, V_GK, V_ROWS = 0, 48, 56, 64, 68, 72, 76, 77, 78

SLOTS = (["ada0", "ada1", "ada2", "ada3", "q", "k", "v", "glu"]
         + [f"{kind}{b}" for b in range(B) for kind in ("mix", "mod")]
         + ["conv", "attn", "out0", "out1"] + [f"fin{n}" for n in range(FT // 2)] + [f"fout{n}" for n in range(KD)])

FILLS = ([f"x{t}" for t in range(8)] + ["c", "ada0", "ss1", "ada1", "vec", "adt0", "ada2", "adt1", "ada3", "adt2", "adt3"]
         + [f"q{t}" for t in range(4)] + [f"sqq{t}" for t in range(4)]
         + ["k0", "k1", "k2", "qs", "k3"] + [f"sqk{t}" for t in range(4)]
         + [f"v{t}" for t in range(4)] + ["kn0", "kn1", "ks", "so", "vn0", "vn1", "vs", "a0", "b0"]
         + ["st0", "st1", "st2", "st3"])
for _b in range(B):
    FILLS += [f"g{2 * _b}", f"ada{4 + _b}", f"g{2 * _b + 1}"]
    if _b == B - 1:
        FILLS += ["ct", "lnm"]
    FILLS.append(f"adt{4 + _b}")
    if _b < B - 2:
        FILLS.append(f"{'ab'[_b % 2]}{_b // 2 + 1}")
FILLS += (["lnv"] + [f"cp{t}" for t in range(8)] + [f"ap{t}" for t in range(8)]
          + [f"o{t}" for t in range(8)] + [f"f{n}" for n in range(2 * FT)]
          + [f"y{t}" for t in range(5)] + ["y00", "y10", "y20"] + [f"y{t}" for t in range(5, 8)] + ["y01", "y11", "y21"])
NUMBER = {name: n for n, name in enumerate(FILLS)}

LAST_FILL = {"q": "q3", "k": "k3", "v": "v3", "glu": "b0", "conv": "cp7", "attn": "ap7", "out0": "o3", "out1": "o7"}
LAST_FILL.update({f"ada{n}": f"ada{n}" for n in range(4)})
for _b in range(B):
    LAST_FILL[f"mix{_b}"] = f"{'ab'[_b % 2]}{_b // 2 + 1}" if _b < B - 2 else f"g{2 * _b + 1}"
    LAST_FILL[f"mod{_b}"] = f"ada{4 + _b}"
LAST_FILL.update({f"fin{n}": f"f{4 * n + 3}" for n in range(FT // 2)})
LAST_FILL.update({f"fout{n}": f"y{n}" for n in range(KD)})


def program(nc, x_prompt, x_sample, cache_k, cache_v, state_conv, page_table, c_prompt, c_sample,
            w_ada, b_ada, g_norm1, w_in, g_q, g_k, w_attn_proj, w_dwconv, b_dwconv,
            g_conv_ln, b_conv_ln, w_conv_proj, w_out, g_norm2, w_ffn_in, w_ffn_out,
            y_prompt, y_sample, k_prompt, v_prompt, conv_prompt, k_sample, v_sample, conv_sample):
    with ExitStack() as ctx:
        def sb(name, shape, dt=F32):
            return ctx.enter_context(nc.sbuf_tensor(name, shape, dt))

        def pb(name):
            return ctx.enter_context(nc.psum_tensor(name, [P, 512], F32))

        def sem(name):
            return ctx.enter_context(nc.semaphore(name))

        wring = sb("wring", [P, RING, SLOT])
        kring = sb("kring", [P, PG, A])
        vring = sb("vring", [P, PG, A])
        prod = sb("prod", [P, PC // 2, A])
        xT = sb("xT", [P, KD, R])
        hT = sb("hT", [P, KD, R])
        qkvT = sb("qkvT", [P, 12, R])
        qT, kT, vT = qkvT[:, 0:4, :], qkvT[:, 4:8, :], qkvT[:, 8:12, :]
        vnat = sb("vnat", [P, 2, A])
        u = sb("u", [P, CT, TAPS - 1 + R])
        cvT = sb("cvT", [P, CT, R])
        gates = sb("gates", [P, 16, R])
        oT = sb("oT", [P, AT, R])
        pr = sb("pr", [P, 384])
        prT = sb("prT", [P, 384])
        snat = sb("snat", [B, A])
        ident = sb("ident", [P, P])
        ones = sb("ones", [P, P])
        halves = sb("halves", [P, P])
        distm = sb("distm", [P, 384])
        slopes = sb("slopes", [P, H])
        dists = sb("dists", [P, PG])
        alib = sb("alib", [P, PG, H])
        lower = sb("lower", [P, NB, NB])
        vt = sb("vt", [P, V_ROWS + TAPS * CT])
        vec = vt[:, 0:V_ROWS]
        taps = vt[:, V_ROWS:].rearrange("p (t c) -> p t c", c=CT)
        modT = sb("modT", [P, 48, B + 1])
        cT = sb("cT", [P, KD, 32])
        gs = sb("gs", [P, KD, B + 1])
        sall = sb("sall", [P, 2, PG, H])
        s1 = sb("s1", [P, PG + 1, H])
        sown = sb("sown", [P, B, H])
        ppad = sb("ppad", [P, PG, 32])
        pvm = sb("pvm", [P, A])
        headof = sb("headof", [P, H])
        mrow = sb("mrow", [P, 2, P])
        eps = sb("eps", [P, 1])
        diag = sb("diag", [H, PG, H])
        gate = sb("gate", [H, NB])
        cmp1 = sb("cmp1", [H, NB, NB])
        cmp2 = sb("cmp2", [H, NB, NB])
        pen = sb("pen", [H, NB, 2, H])
        tiny = sb("tiny", [P, 64])
        m1, nmx, dg, es, rinv, own = (tiny[:, 0:8], tiny[0:H, 8:9], tiny[0:H, 16:24], tiny[:, 24:32],
                                      tiny[:, 32:40], tiny[:, 40:44])
        pmx, psum_, prin = tiny[:, 48:50], tiny[:, 50:52], tiny[:, 52:54]
        cvs = sb("cvs", [P, CT, B])
        pages = sb("pages", [1, B * PG], I32)
        xn = vring[:, 0:6, :].rearrange("p (t k) n -> p t (k n)", t=3)
        cn = vring[0:B + 1, 6:8, :].rearrange("p k n -> p (k n)")
        stn = gates[0:120, 8:12, :].rearrange("p t r -> p (t r)")[:, 0:2 * C].rearrange("p (t n) -> p t n", t=2)
        vecn = vring[0:V_ROWS, 10, 0:P]
        tapn = vring[0:TAPS * CT, 10, P:2 * P]
        ownp = cvT[0:B, 0:2, :].rearrange("p t r -> p (t r)")[:, 0:A]
        fT = kring[:, 0:12, :].rearrange("p a n -> p (a n)")[:, 0:FT * R].rearrange("p (t r) -> p t r", r=R)
        yn = vring[:, 0:6, :].rearrange("p (t k) n -> p t (k n)", t=3)
        knat = oT[:, :, :].rearrange("p t r -> p (t r)")[:, 0:2 * A].rearrange("p (t n) -> p t n", t=2)
        ctn = prod[0:TAPS - 1 + B, 0, :]
        skv = gates[0:B, 2:6, :].rearrange("p t r -> p (t r)")[:, 0:2 * A].rearrange("p (t n) -> p t n", t=2)
        rstd = prT[:, 0:R]
        soq = gates[0:B, 6, 0:2 * B * H].rearrange("p (t n) -> p t n", t=2)
        roots = [gates[:, 12 + t, :] for t in range(4)]
        lnf = kring[:, 0, 0:R]
        lnsq = kring[:, 1:4, :].rearrange("p a n -> p (a n)")[:, 0:CT * R].rearrange("p (t r) -> p t r", r=R)
        tmp2 = cvT
        sq = gates[:, 0:8, :]

        acc = [pb("acc0"), pb("acc1")]
        qbc = [pb("qbc0"), pb("qbc1")]
        chain = pb("chain")
        psS = pb("psS")
        psT = pb("psT")
        psO = pb("psO")

        vec_in, x_in, c_in, st_in, pt_in = sem("vec_in"), sem("x_in"), sem("c_in"), sem("st_in"), sem("pt_in")
        w_full = [sem(f"w_full{n}") for n in range(RING)]
        k_full = [sem(f"k_full{n}") for n in range(CH)]
        v_full = [sem(f"v_full{n}") for n in range(CH)]
        k_used, v_used = sem("k_used"), sem("v_used")
        consts = sem("consts")
        pool_step = sem("pool_step")
        acc_full = sem("acc_full")
        acc_free = [sem("acc_free0"), sem("acc_free1")]
        act_step, dve_step = sem("act_step"), sem("dve_step")
        c_silu, x_sq, h_ready, x_gone = sem("c_silu"), sem("x_sq"), sem("h_ready"), sem("x_gone")
        sq_ready, q_ready, k_ready = sem("sq_ready"), sem("q_ready"), sem("k_ready")
        so_ready, u_ready, nat_ready = sem("so_ready"), sem("u_ready"), sem("nat_ready")
        qsel_ready, qbc_ready = sem("qsel_ready"), sem("qbc_ready")
        scored = sem("scored")
        gs_ready, pen_ready, mask_ready, bias_ready = sem("gs_ready"), sem("pen_ready"), sem("mask_ready"), sem("bias_ready")
        m1_ready, m1t_ready, dg_ready, mb_ready = sem("m1_ready"), sem("m1t_ready"), sem("dg_ready"), sem("mb_ready")
        s2_ready, e_ready, es_ready, tot_ready = sem("s2_ready"), sem("e_ready"), sem("es_ready"), sem("tot_ready")
        p_ready, pvm_ready, pv_ready, o_ready = sem("p_ready"), sem("pvm_ready"), sem("pv_ready"), sem("o_ready")
        st_ready = sem("st_ready")
        ps_ready, pb_ready, pe_ready, pn_ready = sem("ps_ready"), sem("pb_ready"), sem("pe_ready"), sem("pn_ready")
        pt_ready, pc_ready, po_ready, pp_ready = sem("pt_ready"), sem("pc_ready"), sem("po_ready"), sem("pp_ready")
        ln_c, ln_s, cv_ready = sem("ln_c"), sem("ln_s"), sem("cv_ready")
        mix_ready, x2_ready, x2_sq, h2_ready = sem("mix_ready"), sem("x2_ready"), sem("x2_sq"), sem("h2_ready")
        ss2_ready, root2_ready = sem("ss2_ready"), sem("root2_ready")
        silu_ready, f_ready, y_ready = sem("silu_ready"), sem("f_ready"), sem("y_ready")
        stored = sem("stored")

        block = ctx.enter_context(nc.Block())

        def when_full(eng, name):
            eng.wait_ge(acc_full, NUMBER[name] + 1)
            return acc[NUMBER[name] % 2]

        def freed(ins, name):
            return ins.then_inc(acc_free[NUMBER[name] % 2], 1)

        def wait_freed(eng, name):
            eng.wait_ge(acc_free[NUMBER[name] % 2], NUMBER[name] // 2 + 1)

        def load_pages(eng, ring, cache, full, b, c):
            for g in range(PC * c, PC * c + PC):
                page = eng.value_load(pages[0:1, bass.ds(PG * b + g, 1)], min_val=0, max_val=NPHYS - 1)
                eng.dma_start(ring[:, g, :], cache[bass.ds(page, 1)].rearrange("o p h d -> p (o h d)"))\
                    .then_inc(full[c], 16)

        @block.sync
        def _(sp):
            for t in range(2):
                sp.dma_start(xn[:, t, :], x_prompt[0, t * P:(t + 1) * P, :]).then_inc(x_in, 16)
            sp.dma_start(xn[0:B, 2, :], x_sample[:, 0, :]).then_inc(x_in, 16)
            sp.dma_start(pages[:, :], page_table.rearrange("(o b) p -> o (b p)", o=1)).then_inc(pt_in, 16)

            def load(name):
                n = SLOTS.index(name)
                dst = wring[:, n % RING, :]
                if n >= RING:
                    sp.wait_ge(acc_full, NUMBER[LAST_FILL[SLOTS[n - RING]]] + 1)
                full = dst.rearrange("p (k n) -> p k n", k=KD)
                kind, num = name.rstrip("0123456789"), int(name[len(name.rstrip("0123456789")):] or 0)

                def cols(w, c0, n_):
                    return w[:, c0:c0 + n_].rearrange("(k p) n -> p k n", p=P)

                glu0 = 3 * A
                if kind == "ada":
                    parts = [(full, cols(w_ada, 512 * num, 512))]
                elif kind == "mod":
                    parts = [(full, cols(w_ada, 512 * (4 + num), 512))]
                elif kind in ("q", "k", "v"):
                    parts = [(full, cols(w_in, A * "qkv".index(kind), A))]
                elif kind == "glu":
                    parts = [(full[:, :, 0:P], cols(w_in, glu0, P)), (full[:, :, P:2 * P], cols(w_in, glu0 + C, P))]
                elif kind == "mix":
                    parts = [(full[:, :, 0:2 * P], cols(w_in, glu0 + 2 * C + 2 * P * num, 2 * P))]
                    if num < B - 2:
                        parts.append((full[:, :, 2 * P:3 * P], cols(w_in, glu0 + C * (num % 2) + P * (num // 2 + 1), P)))
                elif kind in ("conv", "attn"):
                    w = w_conv_proj if kind == "conv" else w_attn_proj
                    parts = [(dst.rearrange("p (k n) -> p k n", k=4), w.rearrange("(k p) n -> p k n", p=P))]
                elif kind == "out":
                    parts = [(full, cols(w_out, 512 * num, 512))]
                elif kind == "fin":
                    c0 = 256 * num
                    parts = [(full[:, :, 0:256], cols(w_ffn_in, c0, 256)),
                             (full[:, :, 256:512], cols(w_ffn_in, DFF + c0, 256))]
                else:
                    parts = [(dst[:, 0:FT * P].rearrange("p (k n) -> p k n", k=FT), cols(w_ffn_out, P * num, P))]
                if len(parts) == 1:
                    (d, s), half = parts[0], parts[0][0].shape[1] // 2
                    parts = [(d[:, 0:half, :], s[:, 0:half, :]), (d[:, half:, :], s[:, half:, :])]
                for d, s in parts:
                    sp.dma_start(d, s).then_inc(w_full[n % RING], 16)

            def load_k(b, c):
                if b >= 1:
                    sp.wait_ge(k_used, 2 * (CH * (b - 1) + c + 1))
                load_pages(sp, kring, cache_k, k_full, b, c)

            load("ada0")
            load("ada1")
            load("ada2")
            load("ada3")
            load("q")
            sp.wait_ge(pt_in, 16)
            load_k(0, 0)
            load_k(0, 1)
            load("k")
            load_k(0, 2)
            load_k(0, 3)
            load("v")
            load_k(1, 0)
            load("glu")
            load_k(1, 1)
            load("mix0")
            load_k(1, 2)
            load("mod0")
            load_k(1, 3)
            for b in range(B):
                more = b + 2 < B
                if more:
                    load_k(b + 2, 0)
                    load_k(b + 2, 1)
                if b + 1 < B:
                    load(f"mix{b + 1}")
                if more:
                    load_k(b + 2, 2)
                if b + 1 < B:
                    load(f"mod{b + 1}")
                if more:
                    load_k(b + 2, 3)
            for name in SLOTS[SLOTS.index("conv"):]:
                load(name)
            for e in range(2):
                for t in range(3):
                    wait_freed(sp, f"y{t}{e}")
                    half = slice(512 * e, 512 * e + 512)
                    dst = y_prompt[0, t * P:(t + 1) * P, half] if t < 2 else y_sample[:, 0, half]
                    sp.dma_start(dst, yn[0:dst.shape[0], t, half]).then_inc(stored, 16)
            sp.wait_ge(stored, 16 * 15)

        @block.gpsimd
        def _(pool):
            steps = [0]

            def step(ins):
                steps[0] += 1
                ins.then_inc(pool_step, 1)
                pool.wait_ge(pool_step, steps[0])

            g = nc.gpsimd
            step(g.memset(ident[:, :], 0.0))
            g.affine_select(out=ident[:, :], in_=ident[:, :], compare_op=ALU.not_equal, fill=1.0,
                            base=0, pattern=[[-1, P]], channel_multiplier=1).then_inc(consts, 1)
            pool.wait_ge(consts, 1)
            step(g.memset(ones[:, :], 1.0))
            step(g.memset(eps[:, :], EPS))
            step(g.memset(cT[:, :, :], 0.0))
            step(g.memset(halves[:, :], 0.0))
            step(g.memset(halves[0:DH, 0:DH], 1.0))
            g.memset(halves[DH:P, DH:P], 1.0).then_inc(consts, 1)
            pool.wait_ge(consts, 2)
            for r0, a, n in ((V_ADA, b_ada, 48), (V_G1, g_norm1, 8), (V_G2, g_norm2, 8), (V_BDW, b_dwconv, 4),
                             (V_GLN, g_conv_ln, 4), (V_BLN, b_conv_ln, 4)):
                pool.dma_start(vecn[r0:r0 + n, :], a.rearrange("(t p) -> t p", p=P)).then_inc(vec_in, 16)
            for r0, a in ((V_GQ, g_q), (V_GK, g_k)):
                for e in range(2):
                    pool.dma_start(vecn[r0:r0 + 1, DH * e:DH * e + DH], a.rearrange("(o d) -> o d", o=1))\
                        .then_inc(vec_in, 16)
            pool.dma_start(tapn, w_dwconv.rearrange("t o (c p) -> (t o c) p", p=P)).then_inc(vec_in, 16)
            for t in range(2):
                pool.dma_start(stn[:, t, :], state_conv[4 * t:4 * t + 4].rearrange("b t c -> (b t) c")).then_inc(st_in, 16)
            step(g.iota(distm[:, 0:P], pattern=[[-1, P]], base=0, channel_multiplier=1,
                        allow_small_or_imprecise_dtypes=True))
            step(g.iota(distm[:, P:384], pattern=[[-1, 2 * P]], base=P, channel_multiplier=1,
                        allow_small_or_imprecise_dtypes=True))
            step(g.affine_select(out=distm[:, 0:P], in_=distm[:, 0:P], compare_op=ALU.is_ge, fill=FAR,
                                 base=0, pattern=[[-1, P]], channel_multiplier=1))
            step(g.affine_select(out=distm[:, P:384], in_=distm[:, P:384], compare_op=ALU.is_ge, fill=FAR,
                                 base=P, pattern=[[-1, 2 * P]], channel_multiplier=1))
            for h in range(H):
                step(g.memset(slopes[:, h:h + 1], -2.0 ** (-8.0 * (h + 1) / H)))
            step(g.iota(dists[:, :], pattern=[[-P, PG]], base=PAST, channel_multiplier=-1,
                        allow_small_or_imprecise_dtypes=True))
            step(g.tensor_tensor(alib[:, :, :], dists[:, :].unsqueeze(2).to_broadcast([P, PG, H]),
                                 slopes[:, :].unsqueeze(1).to_broadcast([P, PG, H]), ALU.mult))
            step(g.memset(lower[:, :, :], 1.0))
            step(g.affine_select(out=lower[:, :, :], in_=lower[:, :, :], compare_op=ALU.is_gt, fill=0.0,
                                 base=0, pattern=[[1, NB], [-1, NB]], channel_multiplier=0))
            step(g.memset(ppad[:, :, :], 0.0))
            step(g.memset(headof[:, :], 0.0))
            for q in range(4):
                step(g.affine_select(out=headof[32 * q:32 * q + 32, :], in_=headof[32 * q:32 * q + 32, :],
                                     compare_op=ALU.not_equal, fill=1.0, base=0, pattern=[[-1, H]],
                                     channel_multiplier=1))
            g.memset(u[:, :, 0:TAPS - 1], 0.0).then_inc(consts, 1)

            pool.wait_ge(pt_in, 16)

            pool.wait_ge(acc_full, NUMBER["q3"] + 1)
            for b in range(B):
                for c in range(CH):
                    if b >= 1:
                        pool.wait_ge(v_used, CH * (b - 1) + c + 1)
                    load_pages(pool, vring, cache_v, v_full, b, c)

        @block.scalar
        def _(act):
            steps = [0]

            def step(ins):
                steps[0] += 1
                ins.then_inc(act_step, 1)
                act.wait_ge(act_step, steps[0])

            def func(out, in_, f, **kw):
                return nc.scalar.activation(out, in_, f, **kw)

            act.dma_start(cn[0:1, :], c_prompt).then_inc(c_in, 16)
            act.dma_start(cn[1:B + 1, :], c_sample).then_inc(c_in, 16)
            act.wait_ge(c_in, 32)
            func(cn, cn, ACT.Silu).then_inc(c_silu, 1)
            act.wait_ge(consts, 2)
            bank = when_full(act, "c")
            freed(func(cT[:, :, 0:B + 1], bank[:, 0:KD * (B + 1)].rearrange("p (k b) -> p k b", k=KD), ACT.Copy), "c")

            def mod_rows(name, half):
                bank = when_full(act, name)
                freed(func(mrow[:, half, :], bank[:, 0:P], ACT.Copy), name)

            n_sq = 0

            def root(name, n, dst):
                bank = when_full(act, name)
                freed(func(dst, bank[:, 0:R], ACT.Sqrt, scale=1.0 / n, bias=eps[:, :]), name)

            act.dma_start(conv_sample[:, 0:TAPS - 2, :], state_conv[:, 1:TAPS - 1, :]).then_inc(stored, 16)
            for n in range(4):
                if n == 1:
                    root("ss1", D, rstd)
                if n == 2:
                    bank = when_full(act, "vec")
                    freed(func(vt[:, :], bank[:, 0:V_ROWS + TAPS * CT], ACT.Copy), "vec")
                if n >= 2:
                    act.wait_ge(acc_full, NUMBER[f"adt{n - 2}"] + 1)
                mod_rows(f"ada{n}", n % 2)

            def raw(name, t):
                nonlocal n_sq
                bank = when_full(act, f"{name}{t}")
                dst = qkvT[:, "qkv".index(name) * 4 + t, :]
                freed(func(dst, bank[:, 0:R], ACT.Copy), f"{name}{t}")
                if name != "v":
                    wait_freed(act, f"{name}{t}")
                    if n_sq >= 4:
                        act.wait_ge(acc_full, NUMBER[f"sqq{n_sq - 4}"] + 1)
                    func(tmp2[:, n_sq % 4, :], dst, ACT.Square).then_inc(sq_ready, 1)
                    n_sq += 1

            for t in range(4):
                raw("q", t)
            for t in range(4):
                root(f"sqq{t}", DH, roots[t])
            for t in range(4):
                raw("k", t)
                if t == 2:
                    bank = when_full(act, "qs")
                    freed(func(snat[:, :], bank[0:B, :], ACT.Copy), "qs")
            act.wait_ge(q_ready, 4)
            for t in range(4):
                root(f"sqk{t}", DH, roots[t])
            for t in range(4):
                raw("v", t)

            def rows_out(name, dst):
                bank = when_full(act, name)
                freed(func(dst, bank[0:dst.shape[0], :], ACT.Copy), name)

            for name, dst in (("kn0", knat[:, 0, :]), ("kn1", knat[:, 1, :]), ("ks", skv[:, 0, :])):
                rows_out(name, dst)
            bank = when_full(act, "so")
            freed(func(sown[:, :, :].rearrange("p b h -> p (b h)"), bank[:, 0:B * H], ACT.Copy), "so")
            for name, dst in (("vn0", vnat[:, 0, :]), ("vn1", vnat[:, 1, :]), ("vs", skv[:, 1, :])):
                rows_out(name, dst)

            def glu(name, t):
                bank = when_full(act, f"{name}{t}")
                if name == "a":
                    freed(func(u[:, t, TAPS - 1:], bank[:, 0:R], ACT.Copy), f"a{t}")
                else:
                    freed(func(cvT[:, t, :], bank[:, 0:R], ACT.Sigmoid), f"b{t}")

            glu("a", 0)
            glu("b", 0)
            wait_freed(act, "vs")
            wait_freed(act, "vn1")
            for t in range(2):
                act.dma_start(v_prompt[0, t * P:(t + 1) * P].rearrange("p h d -> p (h d)"), vnat[:, t, :]).then_inc(stored, 16)
                act.dma_start(k_prompt[0, t * P:(t + 1) * P].rearrange("p h d -> p (h d)"), knat[:, t, :]).then_inc(stored, 16)
            act.dma_start(k_sample.rearrange("b o h d -> b (o h d)"), skv[:, 0, :]).then_inc(stored, 16)
            act.dma_start(v_sample.rearrange("b o h d -> b (o h d)"), skv[:, 1, :]).then_inc(stored, 16)
            def gate(n):
                bank = when_full(act, f"g{n}")
                freed(func(gates[:, n, :], bank[:, 0:R], ACT.Sigmoid), f"g{n}")

            for b in range(B):
                i, j = b // 2, b % 2
                act.wait_ge(pb_ready, b + 1)
                for t, (c0, c1) in enumerate(((0, P), (P, 384))):
                    func(pr[:, c0:c1], pr[:, c0:c1], ACT.Exp, bias=pmx[:, t:t + 1],
                         accum_out=psum_[:, t:t + 1]).then_inc(pe_ready, 1)
                act.wait_ge(pt_ready, b + 1)
                act.wait_ge(pp_ready, b)
                func(prT[:, :], psT[:, 0:384], ACT.Copy).then_inc(pc_ready, 1)
                act.wait_ge(s2_ready, b + 1)
                func(s1[:, :, :], s1[:, :, :], ACT.Exp).then_inc(e_ready, 1)
                gate(2 * b)
                mod_rows(f"ada{4 + b}", j)
                gate(2 * b + 1)
                if b == B - 1:
                    bank = when_full(act, "ct")
                    freed(func(ctn[:, :], bank[0:TAPS - 1 + B, :], ACT.Copy), "ct")
                if b == 0:
                    act.wait_ge(stored, 16 * 7)
                act.wait_ge(pp_ready, b + 1)
                func(oT[DH * j:DH * j + DH, i, 0:S], psO[DH * j:DH * j + DH, 0:S], ACT.Copy).then_inc(po_ready, 1)
                if b < B - 2:
                    glu("ab"[j], i + 1)

            root("lnv", C, lnf)
            act.wait_ge(ln_s, 1)
            for t in range(CT):
                func(cvT[:, t, :], cvT[:, t, :], ACT.Silu, scale=vec[:, V_GLN + t:V_GLN + t + 1],
                     bias=vec[:, V_BLN + t:V_BLN + t + 1]).then_inc(cv_ready, 1)
            func(es[:, 0:1], eps[:, :], ACT.Sqrt)
            act.wait_ge(ss2_ready, 1)
            func(rstd, chain[:, 0:R], ACT.Sqrt, scale=1.0 / D, bias=eps[:, :]).then_inc(root2_ready, 1)
            for n in range(FT):
                bank = when_full(act, f"f{2 * n}")
                if n >= 2:
                    wait_freed(act, f"f{2 * n - 3}")
                freed(func(tmp2[:, n % 2, :], bank[:, 0:R], ACT.Silu), f"f{2 * n}")
            wait_freed(act, "ct")
            act.dma_start(conv_prompt[0], ctn[0:TAPS - 1, :]).then_inc(stored, 16)
            act.dma_start(conv_sample[:, TAPS - 2, :], ctn[TAPS - 1:, :]).then_inc(stored, 16)
            act.wait_ge(stored, 16 * 9)
            for e in range(2):
                for t in range(3):
                    rows = P if t < 2 else B
                    bank = when_full(act, f"y{t}{e}")
                    freed(func(yn[0:rows, t, 512 * e:512 * e + 512], bank[0:rows, :], ACT.Copy), f"y{t}{e}")

        @block.vector
        def _(dve):
            v = nc.vector
            steps = [0]

            def step(ins):
                steps[0] += 1
                ins.then_inc(dve_step, 1)
                dve.wait_ge(dve_step, steps[0])

            for t in range(KD):
                bank = when_full(dve, f"x{t}")
                freed(v.tensor_copy(xT[:, t, :], bank[:, 0:R]), f"x{t}")
            wait_freed(dve, "x7")
            wait_freed(dve, "x6")
            v.tensor_tensor(hT[:, :, :], xT[:, :, :], xT[:, :, :], ALU.mult).then_inc(x_sq, 1)

            def row_factors(name):
                wait_freed(dve, name)
                step(v.reciprocal(rstd, rstd))

            def modulation(n):
                bank = when_full(dve, f"adt{n}")
                ins = v.tensor_tensor(modT[:, 4 * n:4 * n + 4, :],
                                      bank[:, 0:P].rearrange("p (t b) -> p t b", t=4)[:, :, 0:B + 1],
                                      vec[:, V_ADA + 4 * n:V_ADA + 4 * n + 4].unsqueeze(2).to_broadcast([P, 4, B + 1]),
                                      ALU.add)
                freed(ins, f"adt{n}")

            def norm_scale(g_row, scale):
                step(v.tensor_scalar(gs[:, :, :], modT[:, scale:scale + KD, :], 1.0, None, ALU.add))
                step(v.tensor_tensor(gs[:, :, :], gs[:, :, :],
                                     vec[:, g_row:g_row + KD].unsqueeze(2).to_broadcast([P, KD, B + 1]), ALU.mult))

            def norm(g_row, shift, scale, out_sem):
                norm_scale(g_row, scale)
                step(v.tensor_tensor(hT[:, :, S:R], hT[:, :, S:R], gs[:, :, 1:B + 1], ALU.mult))
                step(v.tensor_tensor(hT[:, :, S:R], hT[:, :, S:R], modT[:, shift:shift + KD, 1:B + 1], ALU.add))
                for t in range(KD):
                    v.tensor_scalar(hT[:, t, 0:S], hT[:, t, 0:S], gs[:, t, 0:1], modT[:, shift + t, 0:1],
                                    ALU.mult, ALU.add).then_inc(out_sem, 1)

            row_factors("ss1")
            step(v.tensor_tensor(hT[:, :, :], xT[:, :, :], rstd[:, :].unsqueeze(1).to_broadcast([P, KD, R]), ALU.mult))
            wait_freed(dve, "vec")
            step(v.tensor_scalar(vec[:, V_GQ:V_GQ + 1], vec[:, V_GQ:V_GQ + 1], DH ** -0.5, None, ALU.mult))
            for n in range(4):
                modulation(n)
            wait_freed(dve, "adt2")
            wait_freed(dve, "adt3")
            norm(V_G1, 0, 8, h_ready)

            def head_norm(name, t):
                wait_freed(dve, f"sq{name}{t}")
                root = roots[t]
                step(v.reciprocal(root, root))
                tile = qkvT[:, "qk".index(name) * 4 + t, :]
                g = V_GQ if name == "q" else V_GK
                v.scalar_tensor_tensor(tile, tile, vec[:, g:g + 1], root, ALU.mult, ALU.mult)\
                    .then_inc(q_ready if name == "q" else k_ready, 1)

            for t in range(4):
                head_norm("q", t)
                dve.wait_ge(q_ready, t + 1)
            def score(b, half):
                dve.wait_ge(k_full[half // 2], 16 * PC * (b + 1))
                if half == 0:
                    dve.wait_ge(qbc_ready, b + 1)
                n = PC // 2
                v.tensor_tensor(prod[:, :, :], kring[:, n * half:n * half + n, :],
                                qbc[b % 2][:, :].unsqueeze(1).to_broadcast([P, n, A]), ALU.mult).then_inc(k_used, 1)
                dve.wait_ge(k_used, 2 * CH * b + half + 1)
                v.tensor_reduce(sall[:, b % 2, n * half:n * half + n, :].rearrange("p g h -> p (g h)"),
                                prod[:, :, :].rearrange("p g (h d) -> p (g h) d", d=DH), AX.X, ALU.add)\
                    .then_inc(scored, 1)
                dve.wait_ge(scored, 2 * CH * b + half + 1)

            for half in range(4):
                score(0, half)
            for t in range(4):
                head_norm("k", t)
                dve.wait_ge(k_ready, t + 1)
            for half in range(4, 6):
                score(0, half)
            wait_freed(dve, "ks")
            step(v.tensor_tensor(ownp, snat[:, :], skv[:, 0, :], ALU.mult))
            step(v.tensor_reduce(soq[:, 0, 0:H], ownp.rearrange("p (h d) -> p h d", d=DH), AX.X, ALU.add))
            v.tensor_tensor(soq[:, 1, :].rearrange("p (b h) -> p b h", b=B),
                            soq[:, 0, 0:H].unsqueeze(1).to_broadcast([B, B, H]),
                            ident[0:B, 0:B].unsqueeze(2).to_broadcast([B, B, H]), ALU.mult).then_inc(so_ready, 1)
            for half in range(6, 8):
                score(0, half)

            def gated_glu(t):
                wait_freed(dve, f"a{t}")
                wait_freed(dve, f"b{t}")
                v.tensor_tensor(u[:, t, TAPS - 1:], u[:, t, TAPS - 1:], cvT[:, t, :], ALU.mult).then_inc(u_ready, 1)
                dve.wait_ge(u_ready, t + 1)

            dve.wait_ge(consts, 3)
            gated_glu(0)
            for t in range(CT):
                bank = when_full(dve, f"st{t}")
                w = taps[:, 0:TAPS - 1, t].unsqueeze(1).to_broadcast([P, B, TAPS - 1])
                scr = cvT[:, 0, 0:B * (TAPS - 1)].rearrange("p (b t) -> p b t", b=B)
                freed(v.tensor_tensor(scr, bank[:, 0:B * (TAPS - 1)].rearrange("p (b t) -> p b t", b=B), w, ALU.mult),
                      f"st{t}")
                wait_freed(dve, f"st{t}")
                step(v.tensor_reduce(cvs[:, t, :], scr, AX.X, ALU.add))

            def samples_convolution():
                w30 = taps[:, TAPS - 1, :].unsqueeze(2).to_broadcast([P, CT, B])
                step(v.tensor_tensor(cvs[:, :, :], cvs[:, :, :],
                                     vec[:, V_BDW:V_BDW + CT].unsqueeze(2).to_broadcast([P, CT, B]), ALU.add))
                step(v.tensor_tensor(cvT[:, :, S:R], u[:, :, TAPS - 1 + S:], w30, ALU.mult))
                v.tensor_tensor(cvT[:, :, S:R], cvT[:, :, S:R], cvs[:, :, :], ALU.add).then_inc(ln_c, 1)

            def center():
                bank = when_full(dve, "lnm")
                freed(v.tensor_scalar(lnf, bank[:, 0:R], 1.0 / C, None, ALU.mult), "lnm")
                wait_freed(dve, "lnm")
                step(v.tensor_tensor(cvT[:, :, :], cvT[:, :, :], lnf.unsqueeze(1).to_broadcast([P, CT, R]),
                                     ALU.subtract))
                v.tensor_tensor(lnsq, cvT[:, :, :], cvT[:, :, :], ALU.mult).then_inc(ln_c, 1)

            def scale_rows():
                wait_freed(dve, "lnv")
                step(v.reciprocal(lnf, lnf))
                v.tensor_tensor(cvT[:, :, :], cvT[:, :, :], lnf.unsqueeze(1).to_broadcast([P, CT, R]), ALU.mult)\
                    .then_inc(ln_s, 1)

            for b in range(B):
                i, j = b // 2, b % 2

                def meanwhile(*halves):
                    for half in halves:
                        if b + 1 < B:
                            score(b + 1, half)

                def convolve(tap0, tap1, tap0_last=TAPS, tap1_last=TAPS):
                    if b == B - 1:
                        tap0, tap1 = tap0_last, tap1_last
                    cv = cvT[:, i, 0:S]
                    for tap in range(tap0, tap1):
                        src, w = u[:, i, tap:tap + S], taps[:, tap, i:i + 1]
                        if tap == 0:
                            step(v.tensor_scalar(cv, src, w, vec[:, V_BDW + i:V_BDW + i + 1], ALU.mult, ALU.add))
                        else:
                            step(v.scalar_tensor_tensor(cv, src, w, cv, ALU.mult, ALU.add))

                dve.wait_ge(gs_ready, b + 1)
                idh = ident[0:H, 0:H].unsqueeze(1)
                step(v.tensor_tensor(diag[:, :, :], chain[0:H, 0:PG * H].rearrange("p (g h) -> p g h", h=H),
                                     idh.to_broadcast([H, PG, H]), ALU.mult))
                step(v.tensor_reduce(gate[:, :], diag[:, :, :].rearrange("p (n e) h -> p n (e h)", e=2),
                                     AX.X, ALU.add))
                gm = gate[:, :].unsqueeze(1).to_broadcast([H, NB, NB])
                gn = gate[:, :].unsqueeze(2).to_broadcast([H, NB, NB])
                step(v.tensor_tensor(cmp1[:, :, :], gm, gn, ALU.is_equal))
                step(v.tensor_tensor(cmp1[:, :, :], cmp1[:, :, :], lower[0:H, :, :], ALU.mult))
                step(v.tensor_tensor(cmp2[:, :, :], gm, gn, ALU.is_gt))
                step(v.tensor_tensor(cmp1[:, :, :], cmp1[:, :, :], cmp2[:, :, :], ALU.add))
                step(v.tensor_reduce(gate[:, :], cmp1[:, :, :], AX.X, ALU.add))
                step(v.tensor_scalar(gate[:, :], gate[:, :], float(TOPK), NEG, ALU.is_ge, ALU.mult))
                v.tensor_tensor(pen[:, :, :, :], gate[:, :].unsqueeze(2).unsqueeze(3).to_broadcast([H, NB, 2, H]),
                                ident[0:H, 0:H].unsqueeze(1).unsqueeze(1).to_broadcast([H, NB, 2, H]), ALU.mult)\
                    .then_inc(pen_ready, 1)
                dve.wait_ge(ps_ready, b + 1)
                dve.wait_ge(pt_ready, b)
                step(v.scalar_tensor_tensor(pr[:, :], distm[:, :], slopes[:, b:b + 1], psS[:, 0:384],
                                            ALU.mult, ALU.add))
                step(v.tensor_reduce(pmx[:, 0:1], pr[:, 0:P], AX.X, ALU.max, negate=True))
                v.tensor_reduce(pmx[:, 1:2], pr[:, P:384], AX.X, ALU.max, negate=True).then_inc(pb_ready, 1)
                dve.wait_ge(mask_ready, b + 1)
                step(v.tensor_tensor(s1[:, 0:PG, :].rearrange("p g h -> p (g h)"),
                                     sall[:, j, :, :].rearrange("p g h -> p (g h)"), chain[:, 0:PG * H], ALU.add))
                step(v.tensor_copy(s1[:, PG, :], sown[:, b, :]))
                v.tensor_reduce(m1, s1[:, :, :].rearrange("p g h -> p h g"), AX.X, ALU.max).then_inc(m1_ready, 1)
                meanwhile(0)
                convolve(0, 0, 16, 21)
                dve.wait_ge(m1t_ready, b + 1)
                step(v.tensor_reduce(nmx, chain[0:H, 0:P], AX.X, ALU.max, negate=True))
                v.tensor_scalar(dg, ident[0:H, 0:H], nmx, None, ALU.mult).then_inc(dg_ready, 1)
                dve.wait_ge(pe_ready, 2 * b + 2)
                step(v.reciprocal(prin, psum_))
                step(v.tensor_scalar(pr[:, 0:P], pr[:, 0:P], prin[:, 0:1], None, ALU.mult))
                v.tensor_scalar(pr[:, P:384], pr[:, P:384], prin[:, 1:2], None, ALU.mult).then_inc(pn_ready, 1)
                meanwhile(1)
                convolve(0, 0, 21, 26)
                dve.wait_ge(mb_ready, b + 1)
                v.tensor_tensor(s1[:, :, :], s1[:, :, :], chain[:, 0:H].unsqueeze(1).to_broadcast([P, PG + 1, H]),
                                ALU.add).then_inc(s2_ready, 1)
                meanwhile(2)
                if j == 0 and i >= 1:
                    gated_glu(i)
                convolve(16 * j, 16 * j + 5, 26, TAPS)
                if b == B - 1:
                    samples_convolution()
                dve.wait_ge(e_ready, b + 1)
                v.tensor_reduce(es, s1[:, 0:PG, :].rearrange("p g h -> p h g"), AX.X, ALU.add).then_inc(es_ready, 1)
                meanwhile(3)
                if b == B - 1:
                    center()
                    modulation(4 + b)
                dve.wait_ge(tot_ready, b + 1)
                step(v.tensor_tensor(rinv, chain[:, 0:H], s1[:, PG, :], ALU.add))
                step(v.reciprocal(rinv, rinv))
                v.tensor_tensor(ppad[:, :, 0:H], s1[:, 0:PG, :], rinv.unsqueeze(1).to_broadcast([P, PG, H]),
                                ALU.mult).then_inc(p_ready, 1)
                step(v.tensor_tensor(s1[:, PG, :], s1[:, PG, :], rinv, ALU.mult))
                for e in range(2):
                    rows = slice(DH * e, DH * e + DH)
                    step(v.tensor_tensor(own[rows, :], s1[rows, PG, e:H:2], vT[rows, :, S + b], ALU.mult))
                meanwhile(4, 5)
                convolve(16 * j + 5, 16 * j + 8)
                if b == B - 1:
                    scale_rows()
                dve.wait_ge(v_used, CH * (b + 1))
                v.tensor_tensor(pvm[:, :].rearrange("p (h d) -> p h d", d=DH),
                                chain[:, :].rearrange("p (h d) -> p h d", d=DH),
                                headof[:, :].unsqueeze(2).to_broadcast([P, H, DH]), ALU.mult).then_inc(pvm_ready, 1)
                meanwhile(6)
                convolve(16 * j + 8, 16 * j + 11)
                dve.wait_ge(pv_ready, b + 1)
                if b == 0:
                    dve.wait_ge(stored, 16 * 7)
                for e in range(2):
                    rows = slice(DH * e, DH * e + DH)
                    v.tensor_tensor(oT[rows, :, S + b], own[rows, :], chain[rows, 0:AT], ALU.add).then_inc(o_ready, 1)
                dve.wait_ge(o_ready, 2 * b + 2)
                meanwhile(7)
                if b < B - 1:
                    modulation(4 + b)
                convolve(16 * j + 11, min(16 * j + 16, TAPS))

            norm_scale(V_G2, 32)
            wait_freed(dve, f"g{2 * B - 1}")
            wait_freed(dve, f"g{2 * B - 2}")
            for t in range(8):
                bank = when_full(dve, f"cp{t}")
                freed(v.tensor_tensor(hT[:, t, :], bank[:, 0:R], gates[:, 8 + t, :], ALU.mult), f"cp{t}")
            for t in range(8):
                bank = when_full(dve, f"ap{t}")
                freed(v.tensor_tensor(qkvT[:, 4 + t % 2, :], bank[:, 0:R], gates[:, t, :], ALU.mult), f"ap{t}")
                wait_freed(dve, f"ap{t}")
                v.tensor_tensor(hT[:, t, :], hT[:, t, :], qkvT[:, 4 + t % 2, :], ALU.add).then_inc(mix_ready, 1)

            def gated_add(name, gt, t, out_sem):
                bank = when_full(dve, name)
                step(v.tensor_tensor(cvs[:, 0, :], bank[:, S:R], modT[:, gt + t, 1:B + 1], ALU.mult))
                freed(v.scalar_tensor_tensor(xT[:, t, 0:S], bank[:, 0:S], modT[:, gt + t, 0:1], xT[:, t, 0:S],
                                             ALU.mult, ALU.add), name)
                v.tensor_tensor(xT[:, t, S:R], xT[:, t, S:R], cvs[:, 0, :], ALU.add).then_inc(out_sem, 1)

            for t in range(8):
                gated_add(f"o{t}", 16, t, x2_ready)
                dve.wait_ge(x2_ready, t + 1)
                wait_freed(dve, f"o{t}")
                v.tensor_tensor(sq[:, t, :], xT[:, t, :], xT[:, t, :], ALU.mult).then_inc(x2_sq, 1)
            dve.wait_ge(root2_ready, 1)
            step(v.reciprocal(rstd, rstd))
            step(v.tensor_tensor(hT[:, :, S:R], xT[:, :, S:R], rstd[:, S:R].unsqueeze(1).to_broadcast([P, KD, B]),
                                 ALU.mult))
            step(v.tensor_tensor(hT[:, :, S:R], hT[:, :, S:R], gs[:, :, 1:B + 1], ALU.mult))
            step(v.tensor_tensor(hT[:, :, S:R], hT[:, :, S:R], modT[:, 24:24 + KD, 1:B + 1], ALU.add))
            for t in range(KD):
                step(v.tensor_tensor(hT[:, t, 0:S], xT[:, t, 0:S], rstd[:, 0:S], ALU.mult))
                v.tensor_scalar(hT[:, t, 0:S], hT[:, t, 0:S], gs[:, t, 0:1], modT[:, 24 + t, 0:1],
                                ALU.mult, ALU.add).then_inc(h2_ready, 1)
            for n in range(FT):
                bank = when_full(dve, f"f{2 * n + 1}")
                wait_freed(dve, f"f{2 * n}")
                freed(v.tensor_tensor(fT[:, n, :], bank[:, 0:R], tmp2[:, n % 2, :], ALU.mult), f"f{2 * n + 1}")
                wait_freed(dve, f"f{2 * n + 1}")
            for t in range(8):
                gated_add(f"y{t}", 40, t, y_ready)
                dve.wait_ge(y_ready, t + 1)

        @block.tensor
        def _(pe):
            mm = nc.tensor.matmul

            def bank_for(name):
                n = NUMBER[name]
                if n >= 2:
                    pe.wait_ge(acc_free[n % 2], n // 2)
                return acc[n % 2]

            def slot_ready(name, k=KD):
                n = SLOTS.index(name)
                pe.wait_ge(w_full[n % RING], 32 * (n // RING + 1))
                width = FT * P if k == FT else SLOT
                return wring[:, n % RING, 0:width].rearrange("p (k n) -> p k n", k=k)

            def product(bank, c0, width, w, tile, src, last_inc=None, cols=None):
                nk = w.shape[1]
                for k in range(nk):
                    ins = mm(bank[:, c0:c0 + width], w[:, k, P * tile:P * tile + P], src[:, k, :],
                             start=k == 0, stop=k == nk - 1)
                return ins

            pe.wait_ge(consts, 1)
            pe.wait_ge(x_in, 48)
            for t in range(KD):
                bank = bank_for(f"x{t}")
                for r in range(2):
                    nc.tensor.transpose(bank[:, P * r:P * r + P], xn[:, r, P * t:P * t + P], ident[:, :])
                nc.tensor.transpose(bank[:, S:R], xn[0:B, 2, P * t:P * t + P], ident[0:B, 0:B]).then_inc(acc_full, 1)
            pe.wait_ge(c_silu, 1)
            bank = bank_for("c")
            n9 = B + 1
            for t in range(KD):
                ins = nc.tensor.transpose(bank[:, n9 * t:n9 * t + n9], cn[:, P * t:P * t + P], ident[0:n9, 0:n9])
            ins.then_inc(acc_full, 1)

            def sums(name, src, nk, lhsT=ones):
                bank = bank_for(name)
                for k in range(nk):
                    ins = mm(bank[:, 0:R], lhsT[:, :], src[:, k, :], start=k == 0, stop=k == nk - 1)
                ins.then_inc(acc_full, 1)

            def modulation(n):
                w = slot_ready(f"ada{n}" if n < 4 else f"mod{n - 4}")
                bank = bank_for(f"ada{n}")
                for kk in range(KD):
                    for t in range(4):
                        ins = mm(bank[32 * t:32 * t + 32, 0:P], cT[:, kk, :], w[:, kk, P * t:P * t + P],
                                 start=kk == 0, stop=kk == KD - 1)
                ins.then_inc(acc_full, 1)

            def mod_turned(n):
                wait_freed(pe, f"ada{n}")
                bank = bank_for(f"adt{n}")
                nc.tensor.transpose(bank[:, 0:P], mrow[:, n % 2, :], ident[:, :]).then_inc(acc_full, 1)

            wait_freed(pe, "c")
            modulation(0)
            pe.wait_ge(consts, 2)
            pe.wait_ge(x_sq, 1)
            sums("ss1", hT, KD)
            modulation(1)
            pe.wait_ge(vec_in, 16 * 11)
            bank = bank_for("vec")
            nc.tensor.transpose(bank[:, 0:V_ROWS], vecn, ident[0:V_ROWS, 0:V_ROWS])
            nc.tensor.transpose(bank[:, V_ROWS:V_ROWS + TAPS * CT], tapn, ident[0:TAPS * CT, 0:TAPS * CT]).then_inc(acc_full, 1)
            mod_turned(0)
            for n in range(2, 4):
                modulation(n)
                mod_turned(n - 1)
            mod_turned(3)

            def tile(name, w, t, src, ready=None, k0=0, k1=KD):
                bank = bank_for(name) if k0 == 0 else acc[NUMBER[name] % 2]
                for k in range(k0, k1):
                    if ready is not None:
                        pe.wait_ge(ready, k + 1)
                    ins = mm(bank[:, 0:R], w[:, k, P * t:P * t + P], src[:, k, :], start=k == 0, stop=k == KD - 1)
                if k1 == KD:
                    ins.then_inc(acc_full, 1)

            def rows(slot, names, src, tiles=None, ready=None):
                w = slot_ready(slot)
                for t, name in zip(tiles or range(len(names)), names):
                    tile(name, w, t, src, ready if name == names[0] else None)

            def to_rows(name, src, c0, n):
                bank = bank_for(name)
                for t in range(4):
                    ins = nc.tensor.transpose(bank[0:n, P * t:P * t + P], src[:, t, c0:c0 + n], ident[:, :])
                ins.then_inc(acc_full, 1)

            def spread_query(b):
                if b >= 2:
                    pe.wait_ge(scored, 2 * CH * (b - 1))
                mm(qbc[b % 2][:, :], ident[0:B, b:b + 1].to_broadcast([B, P]), snat[:, :], start=True, stop=True)\
                    .then_inc(qbc_ready, 1)

            def prompt_scores(h):
                rws, t = slice(DH * (h % 2), DH * (h % 2) + DH), h // 2
                pe.wait_ge(pb_ready, h)
                mm(psS[:, 0:P], qT[rws, t, 0:P], kT[rws, t, 0:P], start=True, stop=True)
                mm(psS[:, P:384], qT[rws, t, P:S], kT[rws, t, 0:S], start=True, stop=True).then_inc(ps_ready, 1)

            rows("q", [f"q{t}" for t in range(4)], hT, ready=h_ready)
            for t in range(4):
                pe.wait_ge(sq_ready, t + 1)
                sums(f"sqq{t}", tmp2[:, t:t + 1, :], 1, halves)
            w = slot_ready("k")
            for t in range(3):
                tile(f"k{t}", w, t, hT)
            pe.wait_ge(q_ready, 4)
            to_rows("qs", qT, S, B)
            tile("k3", w, 3, hT)
            wait_freed(pe, "qs")
            spread_query(0)
            for t in range(4):
                pe.wait_ge(sq_ready, t + 5)
                sums(f"sqk{t}", tmp2[:, t:t + 1, :], 1, halves)
            spread_query(1)
            rows("v", [f"v{t}" for t in range(4)], hT)
            pe.wait_ge(k_ready, 4)
            to_rows("kn0", kT, 0, P)
            to_rows("kn1", kT, P, P)
            to_rows("ks", kT, S, B)
            pe.wait_ge(so_ready, 1)
            bank = bank_for("so")
            mm(bank[:, 0:B * H], ones[0:B, :], soq[:, 1, :], start=True, stop=True).then_inc(acc_full, 1)
            wait_freed(pe, "v2")
            wait_freed(pe, "v3")
            to_rows("vn0", vT, 0, P)
            to_rows("vn1", vT, P, P)
            to_rows("vs", vT, S, B)
            w = slot_ready("glu")
            tile("a0", w, 0, hT)
            tile("b0", w, 1, hT)
            pe.wait_ge(st_in, 32)
            for t in range(CT):
                bank = bank_for(f"st{t}")
                for r in range(2):
                    ins = nc.tensor.transpose(bank[:, 120 * r:120 * r + 120], stn[:, r, P * t:P * t + P], ident[0:120, 0:120])
                ins.then_inc(acc_full, 1)
            prompt_scores(0)

            for b in range(B):
                i, j = b // 2, b % 2
                pe.wait_ge(scored, 2 * CH * (b + 1))
                pe.wait_ge(o_ready, 2 * b)
                mm(chain[0:H, 0:PG * H], ones[:, 0:H], sall[:, j, :, :].rearrange("p g h -> p (g h)"),
                   start=True, stop=True).then_inc(gs_ready, 1)
                pe.wait_ge(pen_ready, b + 1)
                mm(chain[:, 0:PG * H], ident[:, :], alib[:, :, :].rearrange("p g h -> p (g h)"), start=True, stop=False)
                mm(chain[:, 0:PG * H], ones[0:H, :], pen[:, :, :, :].rearrange("p n e h -> p (n e h)"),
                   start=False, stop=True).then_inc(mask_ready, 1)
                pe.wait_ge(m1_ready, b + 1)
                nc.tensor.transpose(chain[0:H, 0:P], m1, ident[:, :]).then_inc(m1t_ready, 1)
                mix = slot_ready(f"mix{b}")
                tile(f"g{2 * b}", mix, 0, hT, k1=4)
                pe.wait_ge(dg_ready, b + 1)
                mm(chain[:, 0:H], ones[0:H, :], dg, start=True, stop=True).then_inc(mb_ready, 1)
                pe.wait_ge(pn_ready, b + 1)
                pe.wait_ge(pc_ready, b)
                for t in range(3):
                    ins = nc.tensor.transpose(psT[:, P * t:P * t + P], pr[:, P * t:P * t + P], ident[:, :])
                ins.then_inc(pt_ready, 1)
                tile(f"g{2 * b}", mix, 0, hT, k0=4)
                modulation(4 + b)
                rws, vcols = slice(DH * j, DH * j + DH), slice(DH * b, DH * b + DH)
                pe.wait_ge(pc_ready, b + 1)
                pe.wait_ge(po_ready, b)
                mm(psO[rws, 0:S], vnat[:, 0, vcols], prT[:, 0:S], start=True, stop=False)
                mm(psO[rws, P:S], vnat[:, 1, vcols], prT[:, S:384], start=False, stop=True).then_inc(pp_ready, 1)
                if b == B - 1:
                    tile(f"g{2 * b + 1}", mix, 1, hT)
                    to_rows("ct", u, S, TAPS - 1 + B)
                    pe.wait_ge(ln_c, 1)
                    sums("lnm", cvT, CT)
                pe.wait_ge(es_ready, b + 1)
                mm(chain[:, 0:H], ones[:, :], es, start=True, stop=True).then_inc(tot_ready, 1)
                if b < B - 1:
                    tile(f"g{2 * b + 1}", mix, 1, hT, k1=5)
                else:
                    mod_turned(4 + b)
                    pe.wait_ge(ln_c, 2)
                    sums("lnv", lnsq, CT)
                pe.wait_ge(p_ready, b + 1)
                for c in range(CH):
                    pe.wait_ge(v_full[c], 16 * PC * (b + 1))
                    for q in range(PC):
                        ins = mm(chain[32 * q:32 * q + 32, :], ppad[:, PC * c + q, :], vring[:, PC * c + q, :],
                                 start=c == 0, stop=c == CH - 1)
                    ins.then_inc(v_used, 1)
                if b < B - 1:
                    tile(f"g{2 * b + 1}", mix, 1, hT, k0=5)
                    mod_turned(4 + b)
                pe.wait_ge(pvm_ready, b + 1)
                for t in range(AT):
                    ins = mm(chain[:, t:t + 1], pvm[:, P * t:P * t + P], ones[:, 0:1], start=True, stop=True)
                ins.then_inc(pv_ready, 1)
                if b + 2 < B:
                    tile(f"{'ab'[j]}{i + 1}", mix, 2, hT)
                if b + 1 < B:
                    prompt_scores(b + 1)
                if b + 2 < B:
                    spread_query(b + 2)

            def square_sum(t):
                pe.wait_ge(x2_sq, t + 1)
                ins = mm(chain[:, 0:R], ones[:, :], sq[:, t, :], start=t == 0, stop=t == KD - 1)
                if t == KD - 1:
                    ins.then_inc(ss2_ready, 1)

            for slot, name, src in (("conv", "cp", cvT), ("attn", "ap", oT)):
                w = slot_ready(slot, 4)
                if name == "cp":
                    pe.wait_ge(cv_ready, CT)
                else:
                    pe.wait_ge(o_ready, 2 * B)
                    pe.wait_ge(po_ready, B)
                for t in range(8):
                    product(bank_for(f"{name}{t}"), 0, R, w, t, src).then_inc(acc_full, 1)
            for t in range(KD):
                tile(f"o{t}", slot_ready("out0" if t < 4 else "out1"), t % 4, hT, ready=mix_ready if t == 0 else None)
                if t >= 1:
                    square_sum(t - 1)
            square_sum(KD - 1)
            for n in range(FT // 2):
                rows(f"fin{n}", [f"f{4 * n + e}" for e in range(4)], hT, tiles=(0, 2, 1, 3),
                     ready=h2_ready if n == 0 else None)
            wait_freed(pe, f"f{2 * FT - 1}")
            for t in range(KD):
                w = slot_ready(f"fout{t}", FT)
                product(bank_for(f"y{t}"), 0, R, w, 0, fT).then_inc(acc_full, 1)
                if t in (4, KD - 1):
                    e = t // 5
                    pe.wait_ge(y_ready, 4 * e + 4)
                    for r in range(3):
                        to_rows(f"y{r}{e}", xT[:, 4 * e:4 * e + 4, :], P * r, P if r < 2 else B)


INS = ["x_prompt", "x_sample", "cache_k", "cache_v", "state_conv", "page_table", "c_prompt", "c_sample",
       "w_ada", "b_ada", "g_norm1", "w_in", "g_q", "g_k", "w_attn_proj", "w_dwconv", "b_dwconv",
       "g_conv_ln", "b_conv_ln", "w_conv_proj", "w_out", "g_norm2", "w_ffn_in", "w_ffn_out"]
OUTS = [("y_prompt", (1, S, D)), ("y_sample", (B, 1, D)), ("k_prompt", (1, S, H, DH)), ("v_prompt", (1, S, H, DH)),
        ("conv_prompt", (1, TAPS - 1, C)), ("k_sample", (B, 1, H, DH)), ("v_sample", (B, 1, H, DH)),
        ("conv_sample", (B, TAPS - 1, C))]


def kernel(**inputs):
    import numpy as np
    import concourse.bacc as bacc
    from concourse.bass_utils import run_bass_kernel_spmd

    nc = bacc.Bacc("TRN2", target_bir_lowering=False, num_devices=1)
    arrays, args = {}, {}
    for name in INS:
        a = np.ascontiguousarray(inputs[name])
        arrays[f"in_{name}"] = a
        args[name] = nc.dram_tensor(f"in_{name}", a.shape, mybir.dt.from_np(a.dtype), kind="ExternalInput").ap()
    for name, shape in OUTS:
        args[name] = nc.dram_tensor(f"out_{name}", shape, F32, kind="ExternalOutput").ap()
    program(nc, **args)
    r = run_bass_kernel_spmd(nc, [arrays], core_ids=[0])
    return tuple(r.results[0][f"out_{name}"] for name, _ in OUTS)
```

```python
from contextlib import ExitStack

import concourse.bass as bass
from concourse import mybir

F32 = mybir.dt.float32
F32R = mybir.dt.float32r
I32 = mybir.dt.int32
ALU = mybir.AluOpType
ACT = mybir.ActivationFunctionType
AX = mybir.AxisListType

P = 128
D = 1024
KD = D // P
S = 256
B = 8
R = S + B
H, DH = 8, 64
A = H * DH
AT = A // P
C = 512
CT = C // P
TAPS = 31
DFF = 2816
FT = DFF // P
PG = 16
CH = 4
PC = PG // CH
NB = 8
TOPK = 3
PAST = PG * P
NPHYS = 160
EPS = 1e-6
NEG = -1e30
FAR = 1e33
SLOT = 4096
RING = 3

V_ADA, V_G1, V_G2, V_BDW, V_GLN, V_BLN, V_GQ, V_GK, V_ROWS = 0, 48, 56, 64, 68, 72, 76, 77, 78

SLOTS = (["ada0", "ada1", "ada2", "ada3", "q", "k", "v", "glu"]
         + ["mix0", "mod4", "mix1", "mix2", "mod5", "mix3", "mix4", "mod6", "mix5", "mix6", "mod7", "mix7"]
         + ["mod8", "mod9", "mod10", "mod11", "conv", "attn", "out0", "out1"]
         + [f"fin{n}" for n in range(FT // 2)] + [f"fout{n}" for n in range(KD)])

FILLS = ([f"x{t}" for t in range(8)] + ["c", "ada0", "ss1", "ada1", "vec", "adt0", "ada2", "adt1", "ada3", "adt2", "adt3"]
         + ["q0", "q1", "sqq0", "q2", "sqq1", "q3", "sqq2", "sqq3", "k0", "qs", "k1", "sqk0", "k2", "sqk1",
            "k3", "sqk2", "sqk3"]
         + [f"v{t}" for t in range(4)] + ["ks", "vn0", "vn1", "vs", "a0", "b0", "so"]
         + ["st0", "st1", "st2", "st3", "kn0", "kn1"])
for _b in range(B):
    FILLS.append(f"g{2 * _b}")
    if _b % 2 == 0:
        FILLS.append(f"ada{4 + _b // 2}")
    FILLS.append(f"g{2 * _b + 1}")
    if _b % 2 == 0:
        FILLS.append(f"adt{4 + _b // 2}")
    if _b < B - 2:
        FILLS.append(f"{'ab'[_b % 2]}{_b // 2 + 1}")
FILLS += ["ct", "lnm", "ada8", "lnv", "adt8", "ada9", "adt9", "ada10", "ada11", "adt10", "adt11"]
FILLS += ([f"cp{t}" for t in range(8)] + [f"ap{t}" for t in range(8)]
          + [f"o{t}" for t in range(8)] + [f"f{n}" for n in range(2 * FT)]
          + [f"y{t}" for t in range(5)] + ["y00", "y10", "y20"] + [f"y{t}" for t in range(5, 8)] + ["y01", "y11", "y21"])
NUMBER = {name: n for n, name in enumerate(FILLS)}

LAST_FILL = {"q": "q3", "k": "k3", "v": "v3", "glu": "b0"}
LAST_FILL.update({f"ada{n}": f"ada{n}" for n in range(4)})
for _b in range(B):
    LAST_FILL[f"mix{_b}"] = f"{'ab'[_b % 2]}{_b // 2 + 1}" if _b < B - 2 else f"g{2 * _b + 1}"
    LAST_FILL[f"mod{4 + _b}"] = f"ada{4 + _b}"

UNITS = ([(f"{name}{t}", slot, t, 0, 4) for name, slot in (("cp", "conv"), ("ap", "attn")) for t in range(8)]
         + [(f"o{t}", f"out{t // 4}", t % 4, 0, KD) for t in range(8)]
         + [(f"f{4 * n + e}", f"fin{n}", (0, 2, 1, 3)[e], 0, KD) for n in range(FT // 2) for e in range(4)]
         + [(f"y{t}", f"fout{t}", 0, k, min(k + 8, FT)) for t in range(KD) for k in range(0, FT, 8)])
UNIT_RING = 4
AHEAD = UNIT_RING - 1
FIRST_OUT, FIRST_FFN = 2 * KD, 3 * KD
LAST_UNIT = {slot: u for u, (_, slot, _, _, _) in enumerate(UNITS)}


def program(nc, x_prompt, x_sample, cache_k, cache_v, state_conv, page_table, c_prompt, c_sample,
            w_ada, b_ada, g_norm1, w_in, g_q, g_k, w_attn_proj, w_dwconv, b_dwconv,
            g_conv_ln, b_conv_ln, w_conv_proj, w_out, g_norm2, w_ffn_in, w_ffn_out,
            y_prompt, y_sample, k_prompt, v_prompt, conv_prompt, k_sample, v_sample, conv_sample):
    with ExitStack() as ctx:
        def sb(name, shape, dt=F32):
            return ctx.enter_context(nc.sbuf_tensor(name, shape, dt))

        def sb_early(name, shape, dt=F32):
            return early.enter_context(nc.sbuf_tensor(name, shape, dt))

        def pb(name):
            return ctx.enter_context(nc.psum_tensor(name, [P, 512], F32))

        def sem(name):
            return ctx.enter_context(nc.semaphore(name))

        wring = sb("wring", [P, RING, SLOT])
        xT = sb("xT", [P, KD, R])
        hT = sb("hT", [P, KD, R])
        cvT = sb("cvT", [P, CT, R])
        pr = sb("pr", [P, 384])
        prT = sb("prT", [P, 384])
        snat = sb("snat", [B, A])
        ident = sb("ident", [P, P])
        ones = sb("ones", [P, P])
        halves = sb("halves", [P, P])
        distm = sb("distm", [P, 384])
        slopes = sb("slopes", [P, H])
        dists = sb("dists", [P, PG])
        alib = sb("alib", [P, PG, H])
        lower = sb("lower", [P, NB, NB])
        vt = sb("vt", [P, V_ROWS + TAPS * CT])
        vec = vt[:, 0:V_ROWS]
        taps = vt[:, V_ROWS:].rearrange("p (t c) -> p t c", c=CT)
        modT = sb("modT", [P, 48, B + 1])
        cT = sb("cT", [P, KD, 32])
        gs = sb("gs", [P, KD, B + 1])
        sall = sb("sall", [P, 2, PG, H])
        s1 = sb("s1", [P, PG + 1, H])
        sown = sb("sown", [P, B, H])
        ppad = sb("ppad", [P, PG, 32])
        pvm = sb("pvm", [P, A])
        headof = sb("headof", [P, H])
        mrow = sb("mrow", [P, 2, P])
        eps = sb("eps", [P, 1])
        diag = sb("diag", [H, PG, H])
        gate = sb("gate", [H, NB])
        cmp1 = sb("cmp1", [H, NB, NB])
        cmp2 = sb("cmp2", [H, NB, NB])
        pen = sb("pen", [H, NB, 2, H])
        tiny = sb("tiny", [P, 64])
        m1, nmx, dg, es, rinv, own = (tiny[:, 0:8], tiny[0:H, 8:9], tiny[0:H, 16:24], tiny[:, 24:32],
                                      tiny[:, 32:40], tiny[:, 40:44])
        pmx, psum_, prin = tiny[:, 48:50], tiny[:, 50:52], tiny[:, 52:54]
        cvs = sb("cvs", [P, CT, B])
        pages = sb("pages", [1, B * PG], I32)
        early = ExitStack()
        vring = sb_early("vring", [P, PG, A])
        kring = sb_early("kring", [P, PG, A])
        prod = sb_early("prod", [P, PC // 2, A])
        qkvT = sb_early("qkvT", [P, 12, R])
        vnat = sb_early("vnat", [P, 2, A])
        u = sb_early("u", [P, CT, TAPS - 1 + R])
        gates = sb_early("gates", [P, 16, R])
        oT = sb_early("oT", [P, AT, R])
        early.close()
        whi = sb("whi", [P, UNIT_RING, 8, P], F32R)
        wlo = sb("wlo", [P, UNIT_RING, 8, P], F32R)
        xhi = sb("xhi", [P, KD, R], F32R)
        xlo = sb("xlo", [P, KD, R], F32R)
        fhi = sb("fhi", [P, FT, R], F32R)
        flo = sb("flo", [P, FT, R], F32R)
        yn = sb("yn", [P, 3, D])
        qT, kT, vT = qkvT[:, 0:4, :], qkvT[:, 4:8, :], qkvT[:, 8:12, :]
        xn = vring[:, 0:6, :].rearrange("p (t k) n -> p t (k n)", t=3)
        cn = vring[0:B + 1, 6:8, :].rearrange("p k n -> p (k n)")
        stn = gates[0:120, 8:12, :].rearrange("p t r -> p (t r)")[:, 0:2 * C].rearrange("p (t n) -> p t n", t=2)
        vecn = vring[0:V_ROWS, 10, 0:P]
        tapn = vring[0:TAPS * CT, 10, P:2 * P]
        ownp = cvT[0:B, 2:4, :].rearrange("p t r -> p (t r)")[:, 0:A]
        knat = oT[:, :, :].rearrange("p t r -> p (t r)")[:, 0:2 * A].rearrange("p (t n) -> p t n", t=2)
        ctn = prod[0:TAPS - 1 + B, 0, :]
        skv = gates[0:B, 2:6, :].rearrange("p t r -> p (t r)")[:, 0:2 * A].rearrange("p (t n) -> p t n", t=2)
        rstd = prT[:, 0:R]
        soq = gates[0:B, 6, 0:2 * B * H].rearrange("p (t n) -> p t n", t=2)
        roots = [gates[:, 12 + t, :] for t in range(4)]
        lnf = kring[:, 0, 0:R]
        lnsq = kring[:, 1:4, :].rearrange("p a n -> p (a n)")[:, 0:CT * R].rearrange("p (t r) -> p t r", r=R)
        tmp2 = cvT
        sq = gates[:, 0:8, :]

        acc = [pb("acc0"), pb("acc1")]
        qbc = [pb("qbc0"), pb("qbc1")]
        chain = pb("chain")
        psS = pb("psS")
        psT = pb("psT")
        psO = pb("psO")

        vec_in, x_in, c_in, st_in, pt_in = sem("vec_in"), sem("x_in"), sem("c_in"), sem("st_in"), sem("pt_in")
        w_full = [sem(f"w_full{n}") for n in range(RING)]
        k_full = [sem(f"k_full{n}") for n in range(CH)]
        v_full = [sem(f"v_full{n}") for n in range(CH)]
        k_used, v_used = sem("k_used"), sem("v_used")
        consts = sem("consts")
        pool_step = sem("pool_step")
        acc_full = sem("acc_full")
        acc_free = [sem("acc_free0"), sem("acc_free1")]
        dve_step = sem("dve_step")
        c_silu, x_sq, h_ready = sem("c_silu"), sem("x_sq"), sem("h_ready")
        sq_ready, q_ready, k_ready = sem("sq_ready"), sem("q_ready"), sem("k_ready")
        so_ready, u_ready = sem("so_ready"), sem("u_ready")
        qbc_ready = sem("qbc_ready")
        scored = sem("scored")
        gs_ready, pen_ready, mask_ready = sem("gs_ready"), sem("pen_ready"), sem("mask_ready")
        m1_ready, m1t_ready, dg_ready, mb_ready = sem("m1_ready"), sem("m1t_ready"), sem("dg_ready"), sem("mb_ready")
        s2_ready, e_ready, es_ready, tot_ready = sem("s2_ready"), sem("e_ready"), sem("es_ready"), sem("tot_ready")
        p_ready, pvm_ready, pv_ready, o_ready = sem("p_ready"), sem("pvm_ready"), sem("pv_ready"), sem("o_ready")
        ps_ready, pb_ready, pe_ready, pn_ready = sem("ps_ready"), sem("pb_ready"), sem("pe_ready"), sem("pn_ready")
        pt_ready, pc_ready, po_ready, pp_ready = sem("pt_ready"), sem("pc_ready"), sem("po_ready"), sem("pp_ready")
        ln_c, ln_s, cv_ready = sem("ln_c"), sem("ln_s"), sem("cv_ready")
        mix_ready, x2_ready, x2_sq, h2_ready = sem("mix_ready"), sem("x2_ready"), sem("x2_sq"), sem("h2_ready")
        rhi_ready, rlo_ready = sem("rhi_ready"), sem("rlo_ready")
        ss2_ready, root2_ready, scaled = sem("ss2_ready"), sem("root2_ready"), sem("scaled")
        whi_ready, wlo_ready, part_used = sem("whi_ready"), sem("wlo_ready"), sem("part_used")
        xhi_ready, xlo_ready = sem("xhi_ready"), sem("xlo_ready")
        f_ready, y_ready = sem("f_ready"), sem("y_ready")
        stored = sem("stored")

        block = ctx.enter_context(nc.Block())

        def when_full(eng, name):
            eng.wait_ge(acc_full, NUMBER[name] + 1)
            return acc[NUMBER[name] % 2]

        def freed(ins, name):
            return ins.then_inc(acc_free[NUMBER[name] % 2], 1)

        def wait_freed(eng, name):
            eng.wait_ge(acc_free[NUMBER[name] % 2], NUMBER[name] // 2 + 1)

        def unit(u):
            _, slot, t, k0, k1 = UNITS[u]
            n, kn = SLOTS.index(slot), FT if slot[:4] == "fout" else 4 if slot in ("conv", "attn") else KD
            width = FT * P if kn == FT else SLOT
            w = wring[:, n % RING, 0:width].rearrange("p (k n) -> p k n", k=kn)[:, k0:k1, P * t:P * t + P]
            return w, u % UNIT_RING, k1 - k0, (w_full[n % RING], 32 * (n // RING + 1))

        def unit_place_free(eng, u):
            if u >= UNIT_RING:
                name, _, _, _, k1 = UNITS[u - UNIT_RING]
                if name[0] == "y" and k1 < FT:
                    parts = sum(1 for x in UNITS[:u - UNIT_RING + 1] if x[0][0] == "y" and x[4] < FT)
                    eng.wait_ge(part_used, parts)
                else:
                    eng.wait_ge(acc_full, NUMBER[name] + 1)

        def load_pages(eng, ring, cache, full, b, c):
            for g in range(PC * c, PC * c + PC):
                page = eng.value_load(pages[0:1, bass.ds(PG * b + g, 1)], min_val=0, max_val=NPHYS - 1)
                eng.dma_start(ring[:, g, :], cache[bass.ds(page, 1)].rearrange("o p h d -> p (o h d)"))\
                    .then_inc(full[c], 16)

        @block.sync
        def _(sp):
            for t in range(2):
                sp.dma_start(xn[:, t, :], x_prompt[0, t * P:(t + 1) * P, :]).then_inc(x_in, 16)
            sp.dma_start(xn[0:B, 2, :], x_sample[:, 0, :]).then_inc(x_in, 16)
            sp.dma_start(pages[:, :], page_table.rearrange("(o b) p -> o (b p)", o=1)).then_inc(pt_in, 16)

            def load(name):
                n = SLOTS.index(name)
                dst = wring[:, n % RING, :]
                if n >= RING:
                    before = SLOTS[n - RING]
                    if before in LAST_UNIT:
                        sp.wait_ge(wlo_ready, LAST_UNIT[before] + 1)
                    else:
                        sp.wait_ge(acc_full, NUMBER[LAST_FILL[before]] + 1)
                full = dst.rearrange("p (k n) -> p k n", k=KD)
                kind, num = name.rstrip("0123456789"), int(name[len(name.rstrip("0123456789")):] or 0)

                def cols(w, c0, n_):
                    return w[:, c0:c0 + n_].rearrange("(k p) n -> p k n", p=P)

                glu0 = 3 * A
                if kind == "ada":
                    parts = [(full, cols(w_ada, 512 * num, 512))]
                elif kind == "mod":
                    parts = [(full, cols(w_ada, 512 * num, 512))]
                elif kind in ("q", "k", "v"):
                    parts = [(full, cols(w_in, A * "qkv".index(kind), A))]
                elif kind == "glu":
                    parts = [(full[:, :, 0:P], cols(w_in, glu0, P)), (full[:, :, P:2 * P], cols(w_in, glu0 + C, P))]
                elif kind == "mix":
                    parts = [(full[:, :, 0:2 * P], cols(w_in, glu0 + 2 * C + 2 * P * num, 2 * P))]
                    if num < B - 2:
                        parts.append((full[:, :, 2 * P:3 * P], cols(w_in, glu0 + C * (num % 2) + P * (num // 2 + 1), P)))
                elif kind in ("conv", "attn"):
                    w = w_conv_proj if kind == "conv" else w_attn_proj
                    parts = [(dst.rearrange("p (k n) -> p k n", k=4), w.rearrange("(k p) n -> p k n", p=P))]
                elif kind == "out":
                    parts = [(full, cols(w_out, 512 * num, 512))]
                elif kind == "fin":
                    c0 = 256 * num
                    parts = [(full[:, :, 0:256], cols(w_ffn_in, c0, 256)),
                             (full[:, :, 256:512], cols(w_ffn_in, DFF + c0, 256))]
                else:
                    parts = [(dst[:, 0:FT * P].rearrange("p (k n) -> p k n", k=FT), cols(w_ffn_out, P * num, P))]
                if len(parts) == 1:
                    (d, s), half = parts[0], parts[0][0].shape[1] // 2
                    parts = [(d[:, 0:half, :], s[:, 0:half, :]), (d[:, half:, :], s[:, half:, :])]
                for d, s in parts:
                    sp.dma_start(d, s).then_inc(w_full[n % RING], 16)

            def load_k(b, c):
                if b >= 1:
                    sp.wait_ge(k_used, 2 * (CH * (b - 1) + c + 1))
                load_pages(sp, kring, cache_k, k_full, b, c)

            load("ada0")
            load("ada1")
            load("ada2")
            load("ada3")
            load("q")
            sp.wait_ge(pt_in, 16)
            load_k(0, 0)
            load_k(0, 1)
            load("k")
            load_k(0, 2)
            load_k(0, 3)
            load("v")
            load_k(1, 0)
            load("glu")
            load_k(1, 1)
            load("mix0")
            load_k(1, 2)
            load("mod4")
            load_k(1, 3)
            for b in range(B):
                more = b + 2 < B
                if more:
                    load_k(b + 2, 0)
                    load_k(b + 2, 1)
                if b + 1 < B:
                    load(f"mix{b + 1}")
                if more:
                    load_k(b + 2, 2)
                if b + 1 < B and b % 2 == 1:
                    load(f"mod{4 + (b + 1) // 2}")
                if more:
                    load_k(b + 2, 3)
            for name in SLOTS[SLOTS.index("mod8"):]:
                load(name)
            for e in range(2):
                for t in range(3):
                    wait_freed(sp, f"y{t}{e}")
                    half = slice(512 * e, 512 * e + 512)
                    dst = y_prompt[0, t * P:(t + 1) * P, half] if t < 2 else y_sample[:, 0, half]
                    sp.dma_start(dst, yn[0:dst.shape[0], t, half]).then_inc(stored, 16)
            sp.wait_ge(stored, 16 * 15)

        @block.gpsimd
        def _(pool):
            steps = [0]

            def step(ins):
                steps[0] += 1
                ins.then_inc(pool_step, 1)
                pool.wait_ge(pool_step, steps[0])

            g = nc.gpsimd
            step(g.memset(ident[:, :], 0.0))
            g.affine_select(out=ident[:, :], in_=ident[:, :], compare_op=ALU.not_equal, fill=1.0,
                            base=0, pattern=[[-1, P]], channel_multiplier=1).then_inc(consts, 1)
            pool.wait_ge(consts, 1)
            step(g.memset(ones[:, :], 1.0))
            step(g.memset(eps[:, :], EPS))
            step(g.memset(cT[:, :, :], 0.0))
            step(g.memset(halves[:, :], 0.0))
            step(g.memset(halves[0:DH, 0:DH], 1.0))
            g.memset(halves[DH:P, DH:P], 1.0).then_inc(consts, 1)
            pool.wait_ge(consts, 2)
            for r0, a, n in ((V_ADA, b_ada, 48), (V_G1, g_norm1, 8), (V_G2, g_norm2, 8), (V_BDW, b_dwconv, 4),
                             (V_GLN, g_conv_ln, 4), (V_BLN, b_conv_ln, 4)):
                pool.dma_start(vecn[r0:r0 + n, :], a.rearrange("(t p) -> t p", p=P)).then_inc(vec_in, 16)
            for r0, a in ((V_GQ, g_q), (V_GK, g_k)):
                for e in range(2):
                    pool.dma_start(vecn[r0:r0 + 1, DH * e:DH * e + DH], a.rearrange("(o d) -> o d", o=1))\
                        .then_inc(vec_in, 16)
            pool.dma_start(tapn, w_dwconv.rearrange("t o (c p) -> (t o c) p", p=P)).then_inc(vec_in, 16)
            for t in range(2):
                pool.dma_start(stn[:, t, :], state_conv[4 * t:4 * t + 4].rearrange("b t c -> (b t) c")).then_inc(st_in, 16)
            step(g.iota(distm[:, 0:P], pattern=[[-1, P]], base=0, channel_multiplier=1,
                        allow_small_or_imprecise_dtypes=True))
            step(g.iota(distm[:, P:384], pattern=[[-1, 2 * P]], base=P, channel_multiplier=1,
                        allow_small_or_imprecise_dtypes=True))
            step(g.affine_select(out=distm[:, 0:P], in_=distm[:, 0:P], compare_op=ALU.is_ge, fill=FAR,
                                 base=0, pattern=[[-1, P]], channel_multiplier=1))
            step(g.affine_select(out=distm[:, P:384], in_=distm[:, P:384], compare_op=ALU.is_ge, fill=FAR,
                                 base=P, pattern=[[-1, 2 * P]], channel_multiplier=1))
            for h in range(H):
                step(g.memset(slopes[:, h:h + 1], -2.0 ** (-8.0 * (h + 1) / H)))
            step(g.iota(dists[:, :], pattern=[[-P, PG]], base=PAST, channel_multiplier=-1,
                        allow_small_or_imprecise_dtypes=True))
            step(g.tensor_tensor(alib[:, :, :], dists[:, :].unsqueeze(2).to_broadcast([P, PG, H]),
                                 slopes[:, :].unsqueeze(1).to_broadcast([P, PG, H]), ALU.mult))
            step(g.memset(lower[:, :, :], 1.0))
            step(g.affine_select(out=lower[:, :, :], in_=lower[:, :, :], compare_op=ALU.is_gt, fill=0.0,
                                 base=0, pattern=[[1, NB], [-1, NB]], channel_multiplier=0))
            step(g.memset(ppad[:, :, :], 0.0))
            step(g.memset(headof[:, :], 0.0))
            for q in range(4):
                step(g.affine_select(out=headof[32 * q:32 * q + 32, :], in_=headof[32 * q:32 * q + 32, :],
                                     compare_op=ALU.not_equal, fill=1.0, base=0, pattern=[[-1, H]],
                                     channel_multiplier=1))
            g.memset(u[:, :, 0:TAPS - 1], 0.0).then_inc(consts, 1)

            pool.wait_ge(pt_in, 16)

            pool.wait_ge(acc_full, NUMBER["q3"] + 1)
            for b in range(B):
                for c in range(CH):
                    if b >= 1:
                        pool.wait_ge(v_used, CH * (b - 1) + c + 1)
                    load_pages(pool, vring, cache_v, v_full, b, c)

        @block.scalar
        def _(act):
            def func(out, in_, f, **kw):
                return nc.scalar.activation(out, in_, f, **kw)

            act.dma_start(cn[0:1, :], c_prompt).then_inc(c_in, 16)
            act.dma_start(cn[1:B + 1, :], c_sample).then_inc(c_in, 16)
            act.wait_ge(c_in, 32)
            func(cn, cn, ACT.Silu).then_inc(c_silu, 1)
            act.wait_ge(consts, 2)
            bank = when_full(act, "c")
            freed(func(cT[:, :, 0:B + 1], bank[:, 0:KD * (B + 1)].rearrange("p (k b) -> p k b", k=KD), ACT.Copy), "c")

            def mod_rows(name, half):
                bank = when_full(act, name)
                freed(func(mrow[:, half, :], bank[:, 0:P], ACT.Copy), name)

            n_sq = 0

            def root(name, n, dst):
                bank = when_full(act, name)
                freed(func(dst, bank[:, 0:R], ACT.Sqrt, scale=1.0 / n, bias=eps[:, :]), name)

            act.dma_start(conv_sample[:, 0:TAPS - 2, :], state_conv[:, 1:TAPS - 1, :]).then_inc(stored, 16)
            for n in range(4):
                if n == 1:
                    root("ss1", D, rstd)
                if n == 2:
                    bank = when_full(act, "vec")
                    freed(func(vt[:, :], bank[:, 0:V_ROWS + TAPS * CT], ACT.Copy), "vec")
                if n >= 2:
                    act.wait_ge(acc_full, NUMBER[f"adt{n - 2}"] + 1)
                mod_rows(f"ada{n}", n % 2)

            def raw(name, t):
                nonlocal n_sq
                bank = when_full(act, f"{name}{t}")
                dst = qkvT[:, "qkv".index(name) * 4 + t, :]
                freed(func(dst, bank[:, 0:R], ACT.Copy), f"{name}{t}")
                if name != "v":
                    wait_freed(act, f"{name}{t}")
                    if n_sq >= 4:
                        act.wait_ge(acc_full, NUMBER[f"sqq{n_sq - 4}"] + 1)
                    func(tmp2[:, n_sq % 4, :], dst, ACT.Square).then_inc(sq_ready, 1)
                    n_sq += 1

            raw("q", 0)
            for t in range(4):
                if t < 3:
                    raw("q", t + 1)
                root(f"sqq{t}", DH, roots[t])
            raw("k", 0)
            bank = when_full(act, "qs")
            freed(func(snat[:, :], bank[0:B, :], ACT.Copy), "qs")
            for t in range(4):
                if t < 3:
                    raw("k", t + 1)
                act.wait_ge(q_ready, t + 1)
                root(f"sqk{t}", DH, roots[t])
            for t in range(4):
                raw("v", t)

            def rows_out(name, dst):
                bank = when_full(act, name)
                freed(func(dst, bank[0:dst.shape[0], :], ACT.Copy), name)

            for name, dst in (("ks", skv[:, 0, :]), ("vn0", vnat[:, 0, :]), ("vn1", vnat[:, 1, :]), ("vs", skv[:, 1, :])):
                rows_out(name, dst)

            def glu(name, t):
                bank = when_full(act, f"{name}{t}")
                if name == "a":
                    freed(func(u[:, t, TAPS - 1:], bank[:, 0:R], ACT.Copy), f"a{t}")
                else:
                    freed(func(cvT[:, t, :], bank[:, 0:R], ACT.Sigmoid), f"b{t}")

            glu("a", 0)
            glu("b", 0)
            bank = when_full(act, "so")
            freed(func(sown[:, :, :].rearrange("p b h -> p (b h)"), bank[:, 0:B * H], ACT.Copy), "so")
            for name, dst in (("kn0", knat[:, 0, :]), ("kn1", knat[:, 1, :])):
                rows_out(name, dst)
            wait_freed(act, "kn0")
            wait_freed(act, "kn1")
            for t in range(2):
                act.dma_start(v_prompt[0, t * P:(t + 1) * P].rearrange("p h d -> p (h d)"), vnat[:, t, :]).then_inc(stored, 16)
                act.dma_start(k_prompt[0, t * P:(t + 1) * P].rearrange("p h d -> p (h d)"), knat[:, t, :]).then_inc(stored, 16)
            act.dma_start(k_sample.rearrange("b o h d -> b (o h d)"), skv[:, 0, :]).then_inc(stored, 16)
            act.dma_start(v_sample.rearrange("b o h d -> b (o h d)"), skv[:, 1, :]).then_inc(stored, 16)

            def gate(n):
                bank = when_full(act, f"g{n}")
                freed(func(gates[:, n, :], bank[:, 0:R], ACT.Sigmoid), f"g{n}")

            for b in range(B):
                i, j = b // 2, b % 2
                act.wait_ge(pb_ready, b + 1)
                for t, (c0, c1) in enumerate(((0, P), (P, 384))):
                    func(pr[:, c0:c1], pr[:, c0:c1], ACT.Exp, bias=pmx[:, t:t + 1],
                         accum_out=psum_[:, t:t + 1]).then_inc(pe_ready, 1)
                act.wait_ge(pt_ready, b + 1)
                act.wait_ge(pp_ready, b)
                func(prT[:, :], psT[:, 0:384], ACT.Copy).then_inc(pc_ready, 1)
                act.wait_ge(s2_ready, b + 1)
                func(s1[:, :, :], s1[:, :, :], ACT.Exp).then_inc(e_ready, 1)
                gate(2 * b)
                if j == 0:
                    mod_rows(f"ada{4 + i}", i % 2)
                gate(2 * b + 1)
                if b == B - 1:
                    bank = when_full(act, "ct")
                    freed(func(ctn[:, :], bank[0:TAPS - 1 + B, :], ACT.Copy), "ct")
                    wait_freed(act, "ct")
                    act.dma_start(conv_prompt[0], ctn[0:TAPS - 1, :]).then_inc(stored, 16)
                    act.dma_start(conv_sample[:, TAPS - 2, :], ctn[TAPS - 1:, :]).then_inc(stored, 16)
                if b == 0:
                    act.wait_ge(stored, 16 * 7)
                act.wait_ge(pp_ready, b + 1)
                func(oT[DH * j:DH * j + DH, i, 0:S], psO[DH * j:DH * j + DH, 0:S], ACT.Copy).then_inc(po_ready, 1)
                if b < B - 2:
                    glu("ab"[j], i + 1)

            mod_rows("ada8", 0)
            root("lnv", C, lnf)
            mod_rows("ada9", 1)
            act.wait_ge(ln_s, 1)
            for t in range(CT):
                func(cvT[:, t, :], cvT[:, t, :], ACT.Silu, scale=vec[:, V_GLN + t:V_GLN + t + 1],
                     bias=vec[:, V_BLN + t:V_BLN + t + 1]).then_inc(cv_ready, 1)
            for t in range(CT):
                act.wait_ge(cv_ready, t + 1)
                func(fhi[:, t, :], cvT[:, t, :], ACT.Copy).then_inc(rhi_ready, 1)
            mod_rows("ada10", 0)
            mod_rows("ada11", 1)

            def split_weights(u):
                if u < len(UNITS):
                    w, place, n, full = unit(u)
                    act.wait_ge(*full)
                    unit_place_free(act, u)
                    func(whi[:, place, 0:n, :], w, ACT.Copy).then_inc(whi_ready, 1)

            def split_row(t, ready):
                act.wait_ge(ready, t + 1)
                func(xhi[:, t, :], hT[:, t, :], ACT.Copy).then_inc(xhi_ready, 1)

            act.wait_ge(v_used, CH * B)
            for n in range(AHEAD):
                split_weights(n)
            act.wait_ge(o_ready, 2 * B)
            act.wait_ge(po_ready, B)
            for t in range(AT):
                func(fhi[:, CT + t, :], oT[:, t, :], ACT.Copy).then_inc(rhi_ready, 1)
            for n_unit, (name, _, _, _, k1) in enumerate(UNITS):
                split_weights(n_unit + AHEAD)
                if name[:2] == "ap" and name != "ap0":
                    split_row(int(name[2:]) - 1, mix_ready)
                if name == "ap7":
                    split_row(KD - 1, mix_ready)
                if name == f"o{KD - 1}":
                    func(es[:, 0:1], eps[:, :], ACT.Sqrt)
                    act.wait_ge(ss2_ready, 1)
                    func(rstd, chain[:, 0:R], ACT.Sqrt, scale=1.0 / D, bias=eps[:, :]).then_inc(root2_ready, 1)
                    for t in range(KD):
                        act.wait_ge(scaled, t + 1)
                        func(hT[:, t, 0:S], hT[:, t, 0:S], ACT.Identity, scale=gs[:, t, 0:1],
                             bias=modT[:, 24 + t, 0:1]).then_inc(h2_ready, 1)
                        split_row(t, h2_ready)
                if name[0] == "f" and int(name[1:]) % 2 == 0:
                    n = int(name[1:]) // 2
                    bank = when_full(act, name)
                    if n >= 2:
                        wait_freed(act, f"f{2 * n - 3}")
                    freed(func(tmp2[:, n % 2, :], bank[:, 0:R], ACT.Silu), name)
                if name in ("y4", "y7") and k1 == FT:
                    e = int(name[1:]) // 5
                    for t in range(3):
                        rows = P if t < 2 else B
                        bank = when_full(act, f"y{t}{e}")
                        freed(func(yn[0:rows, t, 512 * e:512 * e + 512], bank[0:rows, :], ACT.Copy), f"y{t}{e}")

        @block.vector
        def _(dve):
            v = nc.vector
            steps = [0]

            def mark(ins):
                steps[0] += 1
                ins.then_inc(dve_step, 1)
                return steps[0]

            def step(ins):
                dve.wait_ge(dve_step, mark(ins))

            for t in range(KD):
                bank = when_full(dve, f"x{t}")
                freed(v.tensor_copy(xT[:, t, :], bank[:, 0:R]), f"x{t}")
            wait_freed(dve, "x7")
            wait_freed(dve, "x6")
            v.tensor_tensor(hT[:, :, :], xT[:, :, :], xT[:, :, :], ALU.mult).then_inc(x_sq, 1)

            def row_factors(name):
                wait_freed(dve, name)
                step(v.reciprocal(rstd, rstd))

            def modulation(n):
                bank = when_full(dve, f"adt{n}")
                ins = v.tensor_tensor(modT[:, 4 * n:4 * n + 4, :],
                                      bank[:, 0:P].rearrange("p (t b) -> p t b", t=4)[:, :, 0:B + 1],
                                      vec[:, V_ADA + 4 * n:V_ADA + 4 * n + 4].unsqueeze(2).to_broadcast([P, 4, B + 1]),
                                      ALU.add)
                freed(ins, f"adt{n}")

            def norm_scale(g_row, scale):
                step(v.tensor_scalar(gs[:, :, :], modT[:, scale:scale + KD, :], 1.0, None, ALU.add))
                step(v.tensor_tensor(gs[:, :, :], gs[:, :, :],
                                     vec[:, g_row:g_row + KD].unsqueeze(2).to_broadcast([P, KD, B + 1]), ALU.mult))

            def norm(g_row, shift, scale, out_sem):
                norm_scale(g_row, scale)
                step(v.tensor_tensor(hT[:, :, S:R], hT[:, :, S:R], gs[:, :, 1:B + 1], ALU.mult))
                step(v.tensor_tensor(hT[:, :, S:R], hT[:, :, S:R], modT[:, shift:shift + KD, 1:B + 1], ALU.add))
                for t in range(KD):
                    v.tensor_scalar(hT[:, t, 0:S], hT[:, t, 0:S], gs[:, t, 0:1], modT[:, shift + t, 0:1],
                                    ALU.mult, ALU.add).then_inc(out_sem, 1)

            row_factors("ss1")
            step(v.tensor_tensor(hT[:, :, :], xT[:, :, :], rstd[:, :].unsqueeze(1).to_broadcast([P, KD, R]), ALU.mult))
            wait_freed(dve, "vec")
            step(v.tensor_scalar(vec[:, V_GQ:V_GQ + 1], vec[:, V_GQ:V_GQ + 1], DH ** -0.5, None, ALU.mult))
            for n in range(4):
                modulation(n)
            wait_freed(dve, "adt2")
            wait_freed(dve, "adt3")
            norm(V_G1, 0, 8, h_ready)

            def head_norm(name, t):
                wait_freed(dve, f"sq{name}{t}")
                root = roots[t]
                step(v.reciprocal(root, root))
                tile = qkvT[:, "qk".index(name) * 4 + t, :]
                g = V_GQ if name == "q" else V_GK
                v.scalar_tensor_tensor(tile, tile, vec[:, g:g + 1], root, ALU.mult, ALU.mult)\
                    .then_inc(q_ready if name == "q" else k_ready, 1)

            for t in range(4):
                head_norm("q", t)
                dve.wait_ge(q_ready, t + 1)
            def multiply(b, half):
                n = PC // 2
                dve.wait_ge(k_full[half // 2], 16 * PC * (b + 1))
                if half == 0:
                    dve.wait_ge(qbc_ready, b + 1)
                if b or half:
                    dve.wait_ge(scored, 2 * CH * b + half)
                v.tensor_tensor(prod[:, :, :], kring[:, n * half:n * half + n, :],
                                qbc[b % 2][:, :].unsqueeze(1).to_broadcast([P, n, A]), ALU.mult).then_inc(k_used, 1)

            def add_up(b, half):
                n = PC // 2
                dve.wait_ge(k_used, 2 * CH * b + half + 1)
                v.tensor_reduce(sall[:, b % 2, n * half:n * half + n, :].rearrange("p g h -> p (g h)"),
                                prod[:, :, :].rearrange("p g (h d) -> p (g h) d", d=DH), AX.X, ALU.add)\
                    .then_inc(scored, 1)

            def score(b, half):
                multiply(b, half)
                add_up(b, half)

            for half in range(4):
                score(0, half)
            for t in range(4):
                head_norm("k", t)
                dve.wait_ge(k_ready, t + 1)
            for half in range(4, 8):
                score(0, half)
            wait_freed(dve, "ks")
            step(v.tensor_tensor(ownp, snat[:, :], skv[:, 0, :], ALU.mult))
            step(v.tensor_reduce(soq[:, 0, 0:H], ownp.rearrange("p (h d) -> p h d", d=DH), AX.X, ALU.add))
            v.tensor_tensor(soq[:, 1, :].rearrange("p (b h) -> p b h", b=B),
                            soq[:, 0, 0:H].unsqueeze(1).to_broadcast([B, B, H]),
                            ident[0:B, 0:B].unsqueeze(2).to_broadcast([B, B, H]), ALU.mult).then_inc(so_ready, 1)

            gated, tapped, tap_mark = [0], [0], [0]

            def tap(count=1):
                for _ in range(count):
                    if tapped[0] == gated[0] * TAPS:
                        return
                    t, n = divmod(tapped[0], TAPS)
                    cv, src, w = cvT[:, t, 0:S], u[:, t, n:n + S], taps[:, n, t:t + 1]
                    if n == 0:
                        dve.wait_ge(u_ready, t + 1)
                        tap_mark[0] = mark(v.tensor_scalar(cv, src, w, vec[:, V_BDW + t:V_BDW + t + 1],
                                                           ALU.mult, ALU.add))
                    else:
                        dve.wait_ge(dve_step, tap_mark[0])
                        tap_mark[0] = mark(v.scalar_tensor_tensor(cv, src, w, cv, ALU.mult, ALU.add))
                    tapped[0] += 1

            def gated_glu(t):
                wait_freed(dve, f"a{t}")
                wait_freed(dve, f"b{t}")
                v.tensor_tensor(u[:, t, TAPS - 1:], u[:, t, TAPS - 1:], cvT[:, t, :], ALU.mult).then_inc(u_ready, 1)
                gated[0] = t + 1

            dve.wait_ge(consts, 3)
            gated_glu(0)
            dve.wait_ge(u_ready, 1)
            for t in range(CT):
                bank = when_full(dve, f"st{t}")
                w = taps[:, 0:TAPS - 1, t].unsqueeze(1).to_broadcast([P, B, TAPS - 1])
                scr = cvT[:, 0, 0:B * (TAPS - 1)].rearrange("p (b t) -> p b t", b=B)
                freed(v.tensor_tensor(scr, bank[:, 0:B * (TAPS - 1)].rearrange("p (b t) -> p b t", b=B), w, ALU.mult),
                      f"st{t}")
                wait_freed(dve, f"st{t}")
                step(v.tensor_reduce(cvs[:, t, :], scr, AX.X, ALU.add))

            def samples_convolution():
                w30 = taps[:, TAPS - 1, :].unsqueeze(2).to_broadcast([P, CT, B])
                step(v.tensor_tensor(cvs[:, :, :], cvs[:, :, :],
                                     vec[:, V_BDW:V_BDW + CT].unsqueeze(2).to_broadcast([P, CT, B]), ALU.add))
                step(v.tensor_tensor(cvT[:, :, S:R], u[:, :, TAPS - 1 + S:], w30, ALU.mult))
                v.tensor_tensor(cvT[:, :, S:R], cvT[:, :, S:R], cvs[:, :, :], ALU.add).then_inc(ln_c, 1)

            def center():
                bank = when_full(dve, "lnm")
                freed(v.tensor_scalar(lnf, bank[:, 0:R], 1.0 / C, None, ALU.mult), "lnm")
                wait_freed(dve, "lnm")
                step(v.tensor_tensor(cvT[:, :, :], cvT[:, :, :], lnf.unsqueeze(1).to_broadcast([P, CT, R]),
                                     ALU.subtract))
                v.tensor_tensor(lnsq, cvT[:, :, :], cvT[:, :, :], ALU.mult).then_inc(ln_c, 1)

            def scale_rows():
                wait_freed(dve, "lnv")
                step(v.reciprocal(lnf, lnf))
                v.tensor_tensor(cvT[:, :, :], cvT[:, :, :], lnf.unsqueeze(1).to_broadcast([P, CT, R]), ALU.mult)\
                    .then_inc(ln_s, 1)

            for b in range(B):
                i, j = b // 2, b % 2

                def multiply_next(half):
                    if b + 1 < B:
                        multiply(b + 1, half)

                def add_up_next(half):
                    if b + 1 < B:
                        add_up(b + 1, half)

                idh = ident[0:H, 0:H].unsqueeze(1)
                gm = gate[:, :].unsqueeze(1).to_broadcast([H, NB, NB])
                gn = gate[:, :].unsqueeze(2).to_broadcast([H, NB, NB])
                dve.wait_ge(gs_ready, b + 1)
                at_diag = mark(v.tensor_tensor(diag[:, :, :], chain[0:H, 0:PG * H].rearrange("p (g h) -> p g h", h=H),
                                               idh.to_broadcast([H, PG, H]), ALU.mult))
                dve.wait_ge(ps_ready, b + 1)
                dve.wait_ge(pt_ready, b)
                at_pr = mark(v.scalar_tensor_tensor(pr[:, :], distm[:, :], slopes[:, b:b + 1], psS[:, 0:384],
                                                    ALU.mult, ALU.add))
                dve.wait_ge(dve_step, at_diag)
                at_gate = mark(v.tensor_reduce(gate[:, :], diag[:, :, :].rearrange("p (n e) h -> p n (e h)", e=2),
                                               AX.X, ALU.add))
                dve.wait_ge(dve_step, at_pr)
                at_max = mark(v.tensor_reduce(pmx[:, 0:1], pr[:, 0:P], AX.X, ALU.max, negate=True))
                dve.wait_ge(dve_step, at_gate)
                at_same = mark(v.tensor_tensor(cmp1[:, :, :], gm, gn, ALU.is_equal))
                at_higher = mark(v.tensor_tensor(cmp2[:, :, :], gm, gn, ALU.is_gt))
                dve.wait_ge(dve_step, at_same)
                at_first = mark(v.tensor_tensor(cmp1[:, :, :], cmp1[:, :, :], lower[0:H, :, :], ALU.mult))
                v.tensor_reduce(pmx[:, 1:2], pr[:, P:384], AX.X, ALU.max, negate=True).then_inc(pb_ready, 1)
                dve.wait_ge(dve_step, at_first)
                at_count = mark(v.tensor_tensor(cmp1[:, :, :], cmp1[:, :, :], cmp2[:, :, :], ALU.add))
                tap()
                dve.wait_ge(dve_step, at_count)
                at_rank = mark(v.tensor_reduce(gate[:, :], cmp1[:, :, :], AX.X, ALU.add))
                tap()
                dve.wait_ge(dve_step, at_rank)
                at_pen = mark(v.tensor_scalar(gate[:, :], gate[:, :], float(TOPK), NEG, ALU.is_ge, ALU.mult))
                if b == 0:
                    wait_freed(dve, "so")
                mark(v.tensor_copy(s1[:, PG, :], sown[:, b, :]))
                dve.wait_ge(dve_step, at_pen)
                v.tensor_tensor(pen[:, :, :, :], gate[:, :].unsqueeze(2).unsqueeze(3).to_broadcast([H, NB, 2, H]),
                                ident[0:H, 0:H].unsqueeze(1).unsqueeze(1).to_broadcast([H, NB, 2, H]), ALU.mult)\
                    .then_inc(pen_ready, 1)
                multiply_next(0)
                dve.wait_ge(mask_ready, b + 1)
                at_s1 = mark(v.tensor_tensor(s1[:, 0:PG, :].rearrange("p g h -> p (g h)"),
                                             sall[:, j, :, :].rearrange("p g h -> p (g h)"), chain[:, 0:PG * H], ALU.add))
                add_up_next(0)
                dve.wait_ge(dve_step, at_s1)
                v.tensor_reduce(m1, s1[:, :, :].rearrange("p g h -> p h g"), AX.X, ALU.max).then_inc(m1_ready, 1)
                tap()
                multiply_next(1)
                if j == 0 and i >= 1:
                    gated_glu(i)
                tap(7 if b == B - 1 else 1)
                add_up_next(1)
                dve.wait_ge(m1t_ready, b + 1)
                at_nmx = mark(v.tensor_reduce(nmx, chain[0:H, 0:P], AX.X, ALU.max, negate=True))
                dve.wait_ge(pe_ready, 2 * b + 2)
                at_prin = mark(v.reciprocal(prin, psum_))
                dve.wait_ge(dve_step, at_nmx)
                v.tensor_scalar(dg, ident[0:H, 0:H], nmx, None, ALU.mult).then_inc(dg_ready, 1)
                dve.wait_ge(dve_step, at_prin)
                at_pn = mark(v.tensor_scalar(pr[:, 0:P], pr[:, 0:P], prin[:, 0:1], None, ALU.mult))
                dve.wait_ge(dve_step, at_pn)
                v.tensor_scalar(pr[:, P:384], pr[:, P:384], prin[:, 1:2], None, ALU.mult).then_inc(pn_ready, 1)
                multiply_next(2)
                tap(6 if b == B - 1 else 1)
                add_up_next(2)
                dve.wait_ge(mb_ready, b + 1)
                v.tensor_tensor(s1[:, :, :], s1[:, :, :], chain[:, 0:H].unsqueeze(1).to_broadcast([P, PG + 1, H]),
                                ALU.add).then_inc(s2_ready, 1)
                tap()
                multiply_next(3)
                tap(TAPS if b == B - 1 else 1)
                add_up_next(3)
                if b == B - 1:
                    samples_convolution()
                tap()
                dve.wait_ge(e_ready, b + 1)
                v.tensor_reduce(es, s1[:, 0:PG, :].rearrange("p g h -> p h g"), AX.X, ALU.add).then_inc(es_ready, 1)
                if b == B - 1:
                    center()
                multiply_next(4)
                tap()
                add_up_next(4)
                dve.wait_ge(tot_ready, b + 1)
                at_tot = mark(v.tensor_tensor(rinv, chain[:, 0:H], s1[:, PG, :], ALU.add))
                tap()
                dve.wait_ge(dve_step, at_tot)
                at_rinv = mark(v.reciprocal(rinv, rinv))
                multiply_next(5)
                dve.wait_ge(dve_step, at_rinv)
                v.tensor_tensor(ppad[:, :, 0:H], s1[:, 0:PG, :], rinv.unsqueeze(1).to_broadcast([P, PG, H]),
                                ALU.mult).then_inc(p_ready, 1)
                at_pown = mark(v.tensor_tensor(s1[:, PG, :], s1[:, PG, :], rinv, ALU.mult))
                add_up_next(5)
                dve.wait_ge(dve_step, at_pown)
                for e in range(2):
                    rows = slice(DH * e, DH * e + DH)
                    at_own = mark(v.tensor_tensor(own[rows, :], s1[rows, PG, e:H:2], vT[rows, :, S + b], ALU.mult))
                tap()
                multiply_next(6)
                tap()
                add_up_next(6)
                if b == B - 1:
                    scale_rows()
                tap()
                dve.wait_ge(v_used, CH * (b + 1))
                v.tensor_tensor(pvm[:, :].rearrange("p (h d) -> p h d", d=DH),
                                chain[:, :].rearrange("p (h d) -> p h d", d=DH),
                                headof[:, :].unsqueeze(2).to_broadcast([P, H, DH]), ALU.mult).then_inc(pvm_ready, 1)
                if b == B - 1:
                    modulation(8)
                multiply_next(7)
                tap()
                if b == 0:
                    dve.wait_ge(stored, 16 * 7)
                dve.wait_ge(pv_ready, b + 1)
                dve.wait_ge(dve_step, at_own)
                for e in range(2):
                    rows = slice(DH * e, DH * e + DH)
                    v.tensor_tensor(oT[rows, :, S + b], own[rows, :], chain[rows, 0:AT], ALU.add).then_inc(o_ready, 1)
                add_up_next(7)
                if j == 0:
                    modulation(4 + i)
                if b == B - 1:
                    for n in range(9, 12):
                        modulation(n)
                tap()

            wait_freed(dve, "adt8")
            wait_freed(dve, "adt9")
            norm_scale(V_G2, 32)
            wait_freed(dve, f"g{2 * B - 1}")
            wait_freed(dve, f"g{2 * B - 2}")
            def split_weights(u):
                if u < len(UNITS):
                    w, place, n, _ = unit(u)
                    dve.wait_ge(whi_ready, u + 1)
                    v.tensor_tensor(wlo[:, place, 0:n, :], w, whi[:, place, 0:n, :].bitcast(F32), ALU.subtract)\
                        .then_inc(wlo_ready, 1)

            def split_row(t, base):
                dve.wait_ge(xhi_ready, base + t + 1)
                v.tensor_tensor(xlo[:, t, :], hT[:, t, :], xhi[:, t, :].bitcast(F32), ALU.subtract)\
                    .then_inc(xlo_ready, 1)

            def split_branch_rows(t):
                src = cvT[:, t, :] if t < CT else oT[:, t - CT, :]
                dve.wait_ge(rhi_ready, t + 1)
                v.tensor_tensor(flo[:, t, :], src, fhi[:, t, :].bitcast(F32), ALU.subtract).then_inc(rlo_ready, 1)

            for t in range(CT):
                split_branch_rows(t)
            for n in range(AHEAD):
                split_weights(n)
            dve.wait_ge(rlo_ready, CT)
            for t in range(KD):
                split_weights(t + AHEAD)
                if t < AT:
                    split_branch_rows(CT + t)
                bank = when_full(dve, f"cp{t}")
                freed(v.tensor_tensor(hT[:, t, :], bank[:, 0:R], gates[:, 8 + t, :], ALU.mult), f"cp{t}")
            for t in range(KD):
                split_weights(KD + t + AHEAD)
                gated = cvT[:, 2 + t % 2, :]
                bank = when_full(dve, f"ap{t}")
                freed(v.tensor_tensor(gated, bank[:, 0:R], gates[:, t, :], ALU.mult), f"ap{t}")
                wait_freed(dve, f"ap{t}")
                v.tensor_tensor(hT[:, t, :], hT[:, t, :], gated, ALU.add).then_inc(mix_ready, 1)
                if t >= 1:
                    split_row(t - 1, 0)

            def gated_add(name, gt, t, out_sem):
                bank = when_full(dve, name)
                step(v.tensor_tensor(cvs[:, 0, :], bank[:, S:R], modT[:, gt + t, 1:B + 1], ALU.mult))
                freed(v.scalar_tensor_tensor(xT[:, t, 0:S], bank[:, 0:S], modT[:, gt + t, 0:1], xT[:, t, 0:S],
                                             ALU.mult, ALU.add), name)
                v.tensor_tensor(xT[:, t, S:R], xT[:, t, S:R], cvs[:, 0, :], ALU.add).then_inc(out_sem, 1)

            split_row(KD - 1, 0)
            for t in range(8):
                split_weights(FIRST_OUT + t + AHEAD)
                gated_add(f"o{t}", 16, t, x2_ready)
                dve.wait_ge(x2_ready, t + 1)
                wait_freed(dve, f"o{t}")
                v.tensor_tensor(sq[:, t, :], xT[:, t, :], xT[:, t, :], ALU.mult).then_inc(x2_sq, 1)
            dve.wait_ge(root2_ready, 1)
            step(v.reciprocal(rstd, rstd))
            step(v.tensor_tensor(hT[:, :, S:R], xT[:, :, S:R], rstd[:, S:R].unsqueeze(1).to_broadcast([P, KD, B]),
                                 ALU.mult))
            step(v.tensor_tensor(hT[:, :, S:R], hT[:, :, S:R], gs[:, :, 1:B + 1], ALU.mult))
            step(v.tensor_tensor(hT[:, :, S:R], hT[:, :, S:R], modT[:, 24:24 + KD, 1:B + 1], ALU.add))
            for t in range(KD):
                v.tensor_tensor(hT[:, t, 0:S], xT[:, t, 0:S], rstd[:, 0:S], ALU.mult).then_inc(scaled, 1)
                if t >= 1:
                    split_row(t - 1, KD)
            split_row(KD - 1, KD)
            dve.wait_ge(xlo_ready, 2 * KD)
            dve.wait_ge(stored, 16 * 9)
            for n_unit in range(FIRST_FFN, len(UNITS)):
                split_weights(n_unit + AHEAD)
                name, _, _, _, k1 = UNITS[n_unit]
                if name[0] == "f" and int(name[1:]) % 2 == 1:
                    n = int(name[1:]) // 2
                    bank = when_full(dve, name)
                    wait_freed(dve, f"f{2 * n}")
                    freed(v.tensor_tensor(hT[:, n % 2, :], bank[:, 0:R], tmp2[:, n % 2, :], ALU.mult), name)
                    wait_freed(dve, name)
                    step(v.tensor_copy(fhi[:, n, :], hT[:, n % 2, :]))
                    v.tensor_tensor(flo[:, n, :], hT[:, n % 2, :], fhi[:, n, :].bitcast(F32), ALU.subtract)\
                        .then_inc(f_ready, 1)
                    dve.wait_ge(f_ready, n + 1)
                if name[0] == "y" and k1 == FT:
                    t = int(name[1:])
                    gated_add(name, 40, t, y_ready)
                    dve.wait_ge(y_ready, t + 1)

        @block.tensor
        def _(pe):
            mm = nc.tensor.matmul

            def bank_for(name):
                n = NUMBER[name]
                if n >= 2:
                    pe.wait_ge(acc_free[n % 2], n // 2)
                return acc[n % 2]

            def slot_ready(name, k=KD):
                n = SLOTS.index(name)
                pe.wait_ge(w_full[n % RING], 32 * (n // RING + 1))
                width = FT * P if k == FT else SLOT
                return wring[:, n % RING, 0:width].rearrange("p (k n) -> p k n", k=k)

            pe.wait_ge(consts, 1)
            pe.wait_ge(x_in, 48)
            for t in range(KD):
                bank = bank_for(f"x{t}")
                for r in range(2):
                    nc.tensor.transpose(bank[:, P * r:P * r + P], xn[:, r, P * t:P * t + P], ident[:, :])
                nc.tensor.transpose(bank[:, S:R], xn[0:B, 2, P * t:P * t + P], ident[0:B, 0:B]).then_inc(acc_full, 1)
            pe.wait_ge(c_silu, 1)
            bank = bank_for("c")
            n9 = B + 1
            for t in range(KD):
                ins = nc.tensor.transpose(bank[:, n9 * t:n9 * t + n9], cn[:, P * t:P * t + P], ident[0:n9, 0:n9])
            ins.then_inc(acc_full, 1)

            def sums(name, src, nk, lhsT=ones):
                bank = bank_for(name)
                for k in range(nk):
                    ins = mm(bank[:, 0:R], lhsT[:, :], src[:, k, :], start=k == 0, stop=k == nk - 1)
                ins.then_inc(acc_full, 1)

            def modulation(n):
                w = slot_ready(f"ada{n}" if n < 4 else f"mod{n}")
                bank = bank_for(f"ada{n}")
                for kk in range(KD):
                    for t in range(4):
                        ins = mm(bank[32 * t:32 * t + 32, 0:P], cT[:, kk, :], w[:, kk, P * t:P * t + P],
                                 start=kk == 0, stop=kk == KD - 1)
                ins.then_inc(acc_full, 1)

            def mod_turned(n):
                wait_freed(pe, f"ada{n}")
                bank = bank_for(f"adt{n}")
                nc.tensor.transpose(bank[:, 0:P], mrow[:, n % 2, :], ident[:, :]).then_inc(acc_full, 1)

            wait_freed(pe, "c")
            modulation(0)
            pe.wait_ge(consts, 2)
            pe.wait_ge(x_sq, 1)
            sums("ss1", hT, KD)
            modulation(1)
            pe.wait_ge(vec_in, 16 * 11)
            bank = bank_for("vec")
            nc.tensor.transpose(bank[:, 0:V_ROWS], vecn, ident[0:V_ROWS, 0:V_ROWS])
            nc.tensor.transpose(bank[:, V_ROWS:V_ROWS + TAPS * CT], tapn, ident[0:TAPS * CT, 0:TAPS * CT]).then_inc(acc_full, 1)
            mod_turned(0)
            for n in range(2, 4):
                modulation(n)
                mod_turned(n - 1)
            mod_turned(3)

            def tile(name, w, t, src, ready=None, k0=0, k1=KD):
                bank = bank_for(name) if k0 == 0 else acc[NUMBER[name] % 2]
                for k in range(k0, k1):
                    if ready is not None:
                        pe.wait_ge(ready, k + 1)
                    ins = mm(bank[:, 0:R], w[:, k, P * t:P * t + P], src[:, k, :], start=k == 0, stop=k == KD - 1)
                if k1 == KD:
                    ins.then_inc(acc_full, 1)

            def rows(slot, names, src, tiles=None, ready=None):
                w = slot_ready(slot)
                for t, name in zip(tiles or range(len(names)), names):
                    tile(name, w, t, src, ready if name == names[0] else None)

            def to_rows(name, src, c0, n):
                bank = bank_for(name)
                for t in range(4):
                    ins = nc.tensor.transpose(bank[0:n, P * t:P * t + P], src[:, t, c0:c0 + n], ident[:, :])
                ins.then_inc(acc_full, 1)

            def spread_query(b):
                if b >= 2:
                    pe.wait_ge(scored, 2 * CH * (b - 1))
                mm(qbc[b % 2][:, :], ident[0:B, b:b + 1].to_broadcast([B, P]), snat[:, :], start=True, stop=True)\
                    .then_inc(qbc_ready, 1)

            def prompt_scores(h):
                rws, t = slice(DH * (h % 2), DH * (h % 2) + DH), h // 2
                pe.wait_ge(pb_ready, h)
                mm(psS[:, 0:P], qT[rws, t, 0:P], kT[rws, t, 0:P], start=True, stop=True)
                mm(psS[:, P:384], qT[rws, t, P:S], kT[rws, t, 0:S], start=True, stop=True).then_inc(ps_ready, 1)

            def head_sums(name, t):
                pe.wait_ge(sq_ready, t + (1 if name == "q" else 5))
                sums(f"sq{name}{t}", tmp2[:, t:t + 1, :], 1, halves)

            w = slot_ready("q")
            tile("q0", w, 0, hT, ready=h_ready)
            for t in range(1, 4):
                tile(f"q{t}", w, t, hT)
                head_sums("q", t - 1)
            w = slot_ready("k")
            tile("k0", w, 0, hT, k1=2)
            head_sums("q", 3)
            tile("k0", w, 0, hT, k0=2)
            pe.wait_ge(q_ready, 4)
            to_rows("qs", qT, S, B)
            tile("k1", w, 1, hT, k1=3)
            wait_freed(pe, "qs")
            spread_query(0)
            tile("k1", w, 1, hT, k0=3)
            for t in range(2, 4):
                head_sums("k", t - 2)
                tile(f"k{t}", w, t, hT)
            head_sums("k", 2)
            w = slot_ready("v")
            head_sums("k", 3)
            spread_query(1)
            rows("v", [f"v{t}" for t in range(4)], hT)
            pe.wait_ge(k_ready, 4)
            to_rows("ks", kT, S, B)
            wait_freed(pe, "v2")
            wait_freed(pe, "v3")
            to_rows("vn0", vT, 0, P)
            to_rows("vn1", vT, P, P)
            to_rows("vs", vT, S, B)
            w = slot_ready("glu")
            tile("a0", w, 0, hT)
            tile("b0", w, 1, hT)
            pe.wait_ge(so_ready, 1)
            bank = bank_for("so")
            mm(bank[:, 0:B * H], ones[0:B, :], soq[:, 1, :], start=True, stop=True).then_inc(acc_full, 1)
            pe.wait_ge(st_in, 32)
            for t in range(CT):
                bank = bank_for(f"st{t}")
                for r in range(2):
                    ins = nc.tensor.transpose(bank[:, 120 * r:120 * r + 120], stn[:, r, P * t:P * t + P], ident[0:120, 0:120])
                ins.then_inc(acc_full, 1)
            prompt_scores(0)

            for b in range(B):
                i, j = b // 2, b % 2
                pe.wait_ge(scored, 2 * CH * (b + 1))
                pe.wait_ge(o_ready, 2 * b)
                mm(chain[0:H, 0:PG * H], ones[:, 0:H], sall[:, j, :, :].rearrange("p g h -> p (g h)"),
                   start=True, stop=True).then_inc(gs_ready, 1)
                if b == 0:
                    to_rows("kn0", kT, 0, P)
                    to_rows("kn1", kT, P, P)
                if 1 <= b < B - 1:
                    spread_query(b + 1)
                    tile(f"{'ab'[1 - j]}{(b - 1) // 2 + 1}", mix, 2, hT, k0=4)
                pe.wait_ge(pen_ready, b + 1)
                mm(chain[:, 0:PG * H], ident[:, :], alib[:, :, :].rearrange("p g h -> p (g h)"), start=True, stop=False)
                mm(chain[:, 0:PG * H], ones[0:H, :], pen[:, :, :, :].rearrange("p n e h -> p (n e h)"),
                   start=False, stop=True).then_inc(mask_ready, 1)
                pe.wait_ge(m1_ready, b + 1)
                nc.tensor.transpose(chain[0:H, 0:P], m1, ident[:, :]).then_inc(m1t_ready, 1)
                mix = slot_ready(f"mix{b}")
                tile(f"g{2 * b}", mix, 0, hT, k1=4)
                pe.wait_ge(dg_ready, b + 1)
                mm(chain[:, 0:H], ones[0:H, :], dg, start=True, stop=True).then_inc(mb_ready, 1)
                pe.wait_ge(pn_ready, b + 1)
                pe.wait_ge(pc_ready, b)
                for t in range(3):
                    ins = nc.tensor.transpose(psT[:, P * t:P * t + P], pr[:, P * t:P * t + P], ident[:, :])
                ins.then_inc(pt_ready, 1)
                tile(f"g{2 * b}", mix, 0, hT, k0=4)
                if j == 0:
                    modulation(4 + i)
                rws, vcols = slice(DH * j, DH * j + DH), slice(DH * b, DH * b + DH)
                pe.wait_ge(pc_ready, b + 1)
                pe.wait_ge(po_ready, b)
                mm(psO[rws, 0:S], vnat[:, 0, vcols], prT[:, 0:S], start=True, stop=False)
                mm(psO[rws, P:S], vnat[:, 1, vcols], prT[:, S:384], start=False, stop=True).then_inc(pp_ready, 1)
                if b == B - 1:
                    tile(f"g{2 * b + 1}", mix, 1, hT)
                    to_rows("ct", u, S, TAPS - 1 + B)
                    pe.wait_ge(ln_c, 1)
                    sums("lnm", cvT, CT)
                pe.wait_ge(es_ready, b + 1)
                mm(chain[:, 0:H], ones[:, :], es, start=True, stop=True).then_inc(tot_ready, 1)
                if b < B - 1:
                    tile(f"g{2 * b + 1}", mix, 1, hT, k1=5)
                else:
                    modulation(8)
                    pe.wait_ge(ln_c, 2)
                    sums("lnv", lnsq, CT)
                pe.wait_ge(p_ready, b + 1)
                for c in range(CH):
                    pe.wait_ge(v_full[c], 16 * PC * (b + 1))
                    for q in range(PC):
                        ins = mm(chain[32 * q:32 * q + 32, :], ppad[:, PC * c + q, :], vring[:, PC * c + q, :],
                                 start=c == 0, stop=c == CH - 1)
                    ins.then_inc(v_used, 1)
                if b < B - 1:
                    tile(f"g{2 * b + 1}", mix, 1, hT, k0=5)
                    if j == 0:
                        mod_turned(4 + i)
                else:
                    mod_turned(8)
                    modulation(9)
                pe.wait_ge(pvm_ready, b + 1)
                for t in range(AT):
                    ins = mm(chain[:, t:t + 1], pvm[:, P * t:P * t + P], ones[:, 0:1], start=True, stop=True)
                ins.then_inc(pv_ready, 1)
                if b + 1 < B:
                    prompt_scores(b + 1)
                if b + 2 < B:
                    tile(f"{'ab'[j]}{i + 1}", mix, 2, hT, k1=4)

            mod_turned(9)
            modulation(10)
            modulation(11)
            mod_turned(10)
            mod_turned(11)

            def square_sum(t):
                pe.wait_ge(x2_sq, t + 1)
                ins = mm(chain[:, 0:R], ones[:, :], sq[:, t, :], start=t == 0, stop=t == KD - 1)
                if t == KD - 1:
                    ins.then_inc(ss2_ready, 1)

            def split_unit(u, hi, lo, ready=None):
                name, _, _, k0, k1 = UNITS[u]
                place, nk = u % UNIT_RING, {"y": FT, "c": CT, "a": AT}.get(name[0], KD)
                pe.wait_ge(wlo_ready, u + 1)
                bank = bank_for(name) if k0 == 0 else acc[NUMBER[name] % 2]
                for k in range(k0, k1):
                    if ready is not None:
                        pe.wait_ge(ready[0], ready[1] + k + 1)
                    mm(bank[:, 0:R], whi[:, place, k - k0, :], lo[:, k, :], start=k == 0, stop=False)
                    mm(bank[:, 0:R], wlo[:, place, k - k0, :], hi[:, k, :], start=False, stop=False)
                    ins = mm(bank[:, 0:R], whi[:, place, k - k0, :], hi[:, k, :], start=False, stop=k == nk - 1)
                ins.then_inc(acc_full if k1 == nk else part_used, 1)

            for t in range(KD):
                split_unit(t, fhi, flo, (rlo_ready, 0) if t == 0 else None)
            for t in range(KD):
                split_unit(KD + t, fhi[:, CT:, :], flo[:, CT:, :], (rlo_ready, CT) if t == 0 else None)
            for t in range(KD):
                split_unit(FIRST_OUT + t, xhi, xlo, (xlo_ready, 0) if t == 0 else None)
                if t >= 1:
                    square_sum(t - 1)
            square_sum(KD - 1)
            for n in range(FIRST_FFN, FIRST_FFN + 2 * FT):
                split_unit(n, xhi, xlo, (xlo_ready, KD) if n == FIRST_FFN else None)
            for n in range(FIRST_FFN + 2 * FT, len(UNITS)):
                name, _, _, _, k1 = UNITS[n]
                split_unit(n, fhi, flo, (f_ready, 0) if name == "y0" else None)
                if k1 == FT and name in ("y4", "y7"):
                    e = int(name[1:]) // 5
                    pe.wait_ge(y_ready, 4 * e + 4)
                    for r in range(3):
                        to_rows(f"y{r}{e}", xT[:, 4 * e:4 * e + 4, :], P * r, P if r < 2 else B)


INS = ["x_prompt", "x_sample", "cache_k", "cache_v", "state_conv", "page_table", "c_prompt", "c_sample",
       "w_ada", "b_ada", "g_norm1", "w_in", "g_q", "g_k", "w_attn_proj", "w_dwconv", "b_dwconv",
       "g_conv_ln", "b_conv_ln", "w_conv_proj", "w_out", "g_norm2", "w_ffn_in", "w_ffn_out"]
OUTS = [("y_prompt", (1, S, D)), ("y_sample", (B, 1, D)), ("k_prompt", (1, S, H, DH)), ("v_prompt", (1, S, H, DH)),
        ("conv_prompt", (1, TAPS - 1, C)), ("k_sample", (B, 1, H, DH)), ("v_sample", (B, 1, H, DH)),
        ("conv_sample", (B, TAPS - 1, C))]


def kernel(**inputs):
    import numpy as np
    import concourse.bacc as bacc
    from concourse.bass_utils import run_bass_kernel_spmd

    nc = bacc.Bacc("TRN2", target_bir_lowering=False, num_devices=1)
    arrays, args = {}, {}
    for name in INS:
        a = np.ascontiguousarray(inputs[name])
        arrays[f"in_{name}"] = a
        args[name] = nc.dram_tensor(f"in_{name}", a.shape, mybir.dt.from_np(a.dtype), kind="ExternalInput").ap()
    for name, shape in OUTS:
        args[name] = nc.dram_tensor(f"out_{name}", shape, F32, kind="ExternalOutput").ap()
    program(nc, **args)
    r = run_bass_kernel_spmd(nc, [arrays], core_ids=[0])
    return tuple(r.results[0][f"out_{name}"] for name, _ in OUTS)
```
